# Optimizing a Trainium2 kernel written in Bass

```python
import jax, jax.numpy as jnp
from jax import lax
import numpy as np

D_MODEL = 1024
BATCH = 1
SEQ = 512
DEPTH = 2

GLA_HEADS = 4
GLA_DK = D_MODEL // 2
GLA_DV = D_MODEL
GLA_HK = GLA_DK // GLA_HEADS
GLA_HV = GLA_DV // GLA_HEADS
GLA_RANK = 16
GLA_TAU = 16.0
CHUNK = 64
POOL_WIDTH = D_MODEL // 2
POOL_WINDOWS = (2, 4, 8, 16)
POOL_GROUPS = 4
POOL_GW = POOL_WIDTH // POOL_GROUPS
D_FF = 2816
N_BRANCH = 2
N_MOD = 9
IN_SIZES = (GLA_DK, GLA_DK, GLA_DV, GLA_DV, GLA_RANK, POOL_WIDTH, D_MODEL, D_MODEL)
IN_WIDTH = sum(IN_SIZES)
IN_SPLITS = tuple(int(s) for s in np.cumsum(IN_SIZES)[:-1])
ALPHA = (2 * DEPTH) ** 0.25
BETA = (8 * DEPTH) ** -0.25
LN_EPS = 1e-5

kernel_name = "hybrid_gla_pool_macaron_deepnorm"

def layer_norm(x, g, b):
    xf = x.astype(jnp.float32)
    mu = jnp.mean(xf, axis=-1, keepdims=True)
    var = jnp.mean(jnp.square(xf - mu), axis=-1, keepdims=True)
    y = (xf - mu) * lax.rsqrt(var + LN_EPS)
    return (y * g.astype(jnp.float32) + b.astype(jnp.float32)).astype(x.dtype)

def modulate(x, shift, scale):
    return x * (1.0 + scale[:, None, :]) + shift[:, None, :]

def swiglu(h, w_up, w_down):
    gu = h @ w_up
    g, u = jnp.split(gu, 2, axis=-1)
    return (jax.nn.silu(g) * u) @ w_down

def gla_chunked(q, k, v, log_a):
    B, S, H, DK = q.shape
    DV = v.shape[-1]
    N = S // CHUNK

    def chunkify(t):
        return t.reshape(B, N, CHUNK, H, t.shape[-1]).transpose(1, 0, 3, 2, 4)

    q, k, v, log_a = chunkify(q), chunkify(k), chunkify(v), chunkify(log_a)
    b = jnp.cumsum(log_a, axis=-2)
    b_last = b[..., -1:, :]
    q_t = q * jnp.exp(b)
    k_t = k * jnp.exp(-b)
    k_end = k * jnp.exp(b_last - b)
    mask = jnp.tril(jnp.ones((CHUNK, CHUNK), dtype=bool))
    scores = jnp.einsum('nbhid,nbhjd->nbhij', q_t, k_t)
    scores = jnp.where(mask, scores, 0.0)
    o_intra = jnp.einsum('nbhij,nbhjv->nbhiv', scores, v)

    def step(state, inp):
        q_c, k_c, v_c, decay = inp
        o = jnp.einsum('bhid,bhdv->bhiv', q_c, state)
        state = state * decay[:, :, 0, :, None] + jnp.einsum('bhjd,bhjv->bhdv', k_c, v_c)
        return state, o

    s0 = jnp.zeros((B, H, DK, DV), jnp.float32)
    _, o_inter = lax.scan(step, s0, (q_t, k_end, v, jnp.exp(b_last)))
    o = o_intra + o_inter
    return o.transpose(1, 0, 3, 2, 4).reshape(B, S, H, DV)

def causal_multiscale_pool(u):
    B, S, _ = u.shape
    cs = jnp.concatenate([jnp.zeros((B, 1, POOL_WIDTH), u.dtype), jnp.cumsum(u, axis=1)], axis=1)
    pos = jnp.arange(S)
    outs = []
    for gi, w in enumerate(POOL_WINDOWS):
        lo_c, hi_c = gi * POOL_GW, (gi + 1) * POOL_GW
        c = cs[..., lo_c:hi_c]
        lo = jnp.maximum(pos + 1 - w, 0)
        window_sum = c[:, 1:] - c[:, lo]
        count = jnp.minimum(pos + 1, w).astype(u.dtype)
        outs.append(window_sum / count[None, :, None] - u[..., lo_c:hi_c])
    return jnp.stack(outs, axis=2)

def hybrid_mixer(h, w_in, w_alpha, b_alpha, gla_norm_g, w_proj_gla,
                 w_pool, pool_scale, w_proj_pool, w_out):
    B, S, _ = h.shape
    z = h @ w_in
    q, k, v, r, a_lr, u, g_gla, g_pool = jnp.split(z, IN_SPLITS, axis=-1)
    f32 = jnp.float32
    q = (q.astype(f32) * GLA_HK ** -0.5).reshape(B, S, GLA_HEADS, GLA_HK)
    k = k.astype(f32).reshape(B, S, GLA_HEADS, GLA_HK)
    v = v.astype(f32).reshape(B, S, GLA_HEADS, GLA_HV)
    log_a = jax.nn.log_sigmoid((a_lr @ w_alpha + b_alpha).astype(f32)) / GLA_TAU
    log_a = log_a.reshape(B, S, GLA_HEADS, GLA_HK)
    o = gla_chunked(q, k, v, log_a)
    mu = jnp.mean(o, axis=-1, keepdims=True)
    var = jnp.mean(jnp.square(o - mu), axis=-1, keepdims=True)
    o = (o - mu) * lax.rsqrt(var + LN_EPS) * gla_norm_g.astype(f32)
    o = o.reshape(B, S, GLA_DV).astype(h.dtype) * jax.nn.silu(r)
    y_gla = o @ w_proj_gla
    p = causal_multiscale_pool(u.astype(f32)).astype(h.dtype)
    p = jnp.einsum('bsgi,gio->bsgo', p, w_pool).reshape(B, S, POOL_WIDTH) * pool_scale
    y_pool = p @ w_proj_pool
    merged = jax.nn.sigmoid(g_gla) * y_gla + jax.nn.sigmoid(g_pool) * y_pool
    return merged @ w_out

def setup_inputs(seed: int = 0) -> dict:
    key = jax.random.key(seed)
    ks = jax.random.split(key, 24)
    L, D = DEPTH, D_MODEL

    def nrm(k, shape, fan_in, scale=1.0):
        return jax.random.normal(k, shape, jnp.float32) * (scale * fan_in ** -0.5)

    def near_one(k, shape):
        return 1.0 + 0.05 * jax.random.normal(k, shape, jnp.float32)

    def small(k, shape):
        return 0.01 * jax.random.normal(k, shape, jnp.float32)

    return {
        "x": jax.random.normal(ks[0], (BATCH, SEQ, D), jnp.float32),
        "c": jax.random.normal(ks[1], (BATCH, D), jnp.float32),
        "w_ada": nrm(ks[2], (L, D, N_MOD * D), D, 0.1),
        "b_ada": small(ks[3], (L, N_MOD * D)),
        "ffn1_up": nrm(ks[4], (L, D, 2 * D_FF), D),
        "ffn1_down": nrm(ks[5], (L, D_FF, D), D_FF, BETA),
        "w_in": nrm(ks[6], (L, D, IN_WIDTH), D),
        "w_alpha": nrm(ks[7], (L, GLA_RANK, GLA_DK), GLA_RANK),
        "b_alpha": small(ks[8], (L, GLA_DK)),
        "gla_norm_g": near_one(ks[9], (L, GLA_HEADS, GLA_HV)),
        "w_proj_gla": nrm(ks[10], (L, GLA_DV, D), GLA_DV, BETA),
        "w_pool": nrm(ks[11], (L, POOL_GROUPS, POOL_GW, POOL_GW), POOL_GW),
        "pool_scale": near_one(ks[12], (L, POOL_WIDTH)),
        "w_proj_pool": nrm(ks[13], (L, POOL_WIDTH, D), POOL_WIDTH, BETA),
        "w_out": nrm(ks[14], (L, D, D), D, BETA),
        "ffn2_up": nrm(ks[15], (L, D, 2 * D_FF), D),
        "ffn2_down": nrm(ks[16], (L, D_FF, D), D_FF, BETA),
        "ln_g": near_one(ks[17], (L, 3, D)),
        "ln_b": small(ks[18], (L, 3, D)),
    }

def reference(x, c, w_ada, b_ada, ffn1_up, ffn1_down, w_in, w_alpha, b_alpha,
              gla_norm_g, w_proj_gla, w_pool, pool_scale, w_proj_pool, w_out,
              ffn2_up, ffn2_down, ln_g, ln_b):
    c_act = jax.nn.silu(c)
    for l in range(DEPTH):
        mod = c_act @ w_ada[l] + b_ada[l]
        sh1, sc1, gt1, sh2, sc2, gt2, sh3, sc3, gt3 = jnp.split(mod, N_MOD, axis=-1)
        h = modulate(x, sh1, sc1)
        y = swiglu(h, ffn1_up[l], ffn1_down[l])
        x = layer_norm(ALPHA * x + 0.5 * (1.0 + gt1[:, None, :]) * y, ln_g[l, 0], ln_b[l, 0])
        h = modulate(x, sh2, sc2)
        y = hybrid_mixer(h, w_in[l], w_alpha[l], b_alpha[l], gla_norm_g[l], w_proj_gla[l],
                         w_pool[l], pool_scale[l], w_proj_pool[l], w_out[l])
        x = layer_norm(ALPHA * x + (1.0 + gt2[:, None, :]) * y, ln_g[l, 1], ln_b[l, 1])
        h = modulate(x, sh3, sc3)
        y = swiglu(h, ffn2_up[l], ffn2_down[l])
        x = layer_norm(ALPHA * x + 0.5 * (1.0 + gt3[:, None, :]) * y, ln_g[l, 2], ln_b[l, 2])
    return x


_drawn_inputs = setup_inputs


def setup_inputs(seed=0):
    import zlib

    import numpy as np

    out = dict(_drawn_inputs(seed))
    spreads = {}
    factors = {'b_ada': 8.0, 'w_alpha': 6.421, 'b_alpha': 64.0, 'gla_norm_g': 8.0, 'pool_scale': 8.0}
    for name, (base, spread) in spreads.items():
        noise = np.random.default_rng([zlib.crc32(name.encode()), seed]).standard_normal(out[name].shape)
        drawn = base * np.exp(spread * noise) if base else spread * noise
        out[name] = __import__('jax').numpy.asarray(drawn.astype(out[name].dtype))
    for name, factor in factors.items():
        out[name] = (out[name] * factor).astype(out[name].dtype)
    return out
```

```python
from contextlib import ExitStack

import concourse.bass as bass
from concourse import mybir

F32 = mybir.dt.float32
F32R = mybir.dt.float32r
I32 = mybir.dt.int32
ACT = mybir.ActivationFunctionType
ALU = mybir.AluOpType

P = 128
D = 1024
S = 512
DEPTH = 2
D_FF = 2816
DK = 512
HEADS = 4
DV = 1024
HV = DV // HEADS
RANK = 16
TAU = 16.0
CHUNK = 64
N_CHUNK = S // CHUNK
PAIRS = S // P
POOL_W = 512
POOL_GROUPS = 4
N_MOD = 9
ALPHA = (2 * DEPTH) ** 0.25
LN_EPS = 1e-5

KT = D // P
FT = D_FF // P
TILE_N = 4
SLOT = 4 * 512
HALF_SLOT = 2 * 512
NARROW = KT * RANK
SMALL = POOL_GROUPS * P

COL_Q, COL_K, COL_V, COL_R = 0, DK, 2 * DK, 2 * DK + DV
COL_A = COL_R + DV
COL_U = COL_A + RANK
COL_GG = COL_U + POOL_W
COL_GP = COL_GG + D

UP_GROUPS = FT // 2
UP_BLOCKS = 2
DOWN_KS = (4, 4, 2, 4, 4, 4)
DOWN_GROUPS = D // 512
DOWN_BLOCKS = len(DOWN_KS)
STAGE_BLOCKS = UP_GROUPS * UP_BLOCKS + DOWN_GROUPS * DOWN_BLOCKS
FFN_GROUPS = UP_GROUPS + DOWN_GROUPS
DOWN0 = UP_GROUPS * UP_BLOCKS
NB = 3 * STAGE_BLOCKS
MIX_GROUPS = 19
GROUP0 = (0, FFN_GROUPS, FFN_GROUPS + MIX_GROUPS)
NG = 2 * FFN_GROUPS + MIX_GROUPS

MIX = [
    ("q", 2, SLOT, 1), ("k", 2, SLOT, 2), ("a", 1, NARROW, None), ("z", 0, 0, None),
    ("v0", 2, SLOT, 3), ("v1", 2, SLOT, 4), ("r0", 2, SLOT, 5), ("r1", 2, SLOT, 6),
    ("u", 2, SLOT, 7), ("gg0", 2, SLOT, 8), ("wp", 1, SMALL, None), ("yg0", 2, SLOT, 9),
    ("gp0", 2, SLOT, 10), ("yp0", 1, SLOT, None), ("gg1", 2, SLOT, 11), ("yg1", 2, SLOT, None),
    ("gp1", 2, SLOT, None), ("yp1", 1, SLOT, None), ("out0", 2, SLOT, None), ("out1", 2, SLOT, None),
]
MIX_FIRST = {}
MIX_GROUP = {}
_b = _g = 0
for _name, _n, _, _ in MIX:
    MIX_FIRST[_name], MIX_GROUP[_name] = _b, _g
    _b += _n
    _g += _name != "a"
assert _b == STAGE_BLOCKS and _g == MIX_GROUPS
MIX_SIZE = [size for _, n, size, _ in MIX for _ in range(n)] + [SLOT]

ADA = 3 * KT
ADA_PAIRS = ADA // 2

PREP_DVE = ("min", "nabs", "log_a", "b", "to_end", "kend", "qt", "decay", "kt")
PREP_ACT = ("exp", "ln", "exp_b", "exp_nb", "exp_end")
STATE_PE = ("kT", "sc") + tuple(f"kv{c}" for c in range(N_CHUNK - 1))
STATE_DVE = ("sc",) + tuple(f"S{c}" for c in range(1, N_CHUNK))
OUT_PE = ("o0", "o1", "sum", "sq")
NORM_ACT = ("o0", "o1", "q0", "q1", "mean", "msq", "sqrt")
NORM_DVE = ("osum", "sqsum", "var", "veps", "rec", "c0", "n0", "g0", "c1", "n1", "g1", "lo0", "lo1")
LN_PE = ("sum", "sq")
LN_ACT = ("msq", "mean", "sqrt") + tuple(f"{w}{t}" for t in range(KT) for w in ("hi", "x"))
LN_DVE = ("var", "veps", "c0", "rec", "n0", "h0") + tuple(f"{w}{t}" for t in range(1, KT) for w in "cnh")
COEF = ("mods", "gate", "scale1", "gs", "bs1", "bs", "lg", "lb")
WINDOWS = tuple(2 << g for g in range(POOL_GROUPS))
WINDOW_STEPS = sum(2 * (g + 1) + 3 for g in range(POOL_GROUPS))


def gla_slot(i):
    h, r = divmod(i, 4)
    steps = [[("o0", h - 1), ("kT", h)], [("o1", h - 1), ("sc", h), ("kv0", h)], [("kv1", h), ("kv2", h)],
             [("kv3", h), ("kv4", h), ("kv5", h), ("kv6", h), ("stats", h - 1)]][r]
    return [(w, n) for w, n in steps if 0 <= n < HEADS]


GLA_GROUPS = {"r0": 0, "r1": 8, "u": 16}


def at(turn, steps, name):
    return turn * len(steps) + steps.index(name) + 1


def trunk(nc, x, c, w_ada, b_ada, ffn1_up, ffn1_down, w_in, w_alpha, b_alpha, gla_norm_g,
          w_proj_gla, w_pool, pool_scale, w_proj_pool, w_out, ffn2_up, ffn2_down, ln_g, ln_b, out):
    with ExitStack() as ctx:
        def sb(name, shape, dt=F32):
            return ctx.enter_context(nc.sbuf_tensor(name, shape, dt))

        def sem(name):
            return ctx.enter_context(nc.semaphore(name))

        def overlay(*specs):
            with ExitStack() as scope:
                return [scope.enter_context(nc.sbuf_tensor(n, s, dt)) for n, s, dt in specs]

        raw = sb("raw", [P, 2, SLOT])
        wh = sb("wh", [P, 2, SLOT], F32R)
        wl = sb("wl", [P, 2, SLOT], F32R)
        xT = sb("xT", [P, KT, S])
        ada = sb("ada", [P, 2, KT, P])
        alpha_w = sb("alpha_w", [RANK, DK])
        ones = sb("ones", [P, P])
        ident = sb("ident", [P, P])
        params = sb("params", [P, P])
        bias = sb("bias", [P, DEPTH * N_MOD * KT + 2 * KT])
        c_act = sb("c_act", [P, KT])
        cinv = sb("cinv", [P, WINDOWS[-1]])
        mods = sb("mods", [P, ADA])
        scale1 = sb("scale1", [P, KT])
        gate = sb("gate", [P, KT])
        gs = sb("gs", [P, KT])
        bs = sb("bs", [P, KT])
        lg = sb("lg", [P, KT])
        lb = sb("lb", [P, KT])
        layer_p = sb("layer_p", [P, KT + 2 * POOL_GROUPS])
        decay = sb("decay", [P, HEADS, N_CHUNK])
        touch = sb("touch", [P, 1])
        touch_v = sb("touch_v", [P, 1])
        mask = sb("mask", [P, P], mybir.dt.uint8)
        ln_acc, ln_accq, ln_sq = overlay(
            ("ln_acc", [P, S], F32), ("ln_accq", [P, S], F32), ("ln_sq", [P, 2, S], F32))
        h_hi = sb("h_hi", [P, KT, S], F32R)
        h_lo = sb("h_lo", [P, KT, S], F32R)
        x_tok, ada_start, stage_rows, maskf = overlay(
            ("x_tok", [P, PAIRS, D], F32), ("ada_start", [P, 4, KT, 512], F32),
            ("stage_rows", [P, 3, P], F32), ("maskf", [P, P], F32))
        _, out_tok = overlay(("gap4", [P, KT, S], F32), ("out_tok", [P, PAIRS, D], F32))
        mean, rstd, ln_tmp, ln_n, ln_h = overlay(
            ("mean", [P, S], F32), ("rstd", [P, S], F32), ("ln_tmp", [P, S], F32),
            ("ln_n", [P, 2, S], F32), ("ln_h", [P, 2, S], F32))
        act_hi, act_lo, silu = overlay(
            ("act_hi", [P, FT, S], F32R), ("act_lo", [P, FT, S], F32R), ("silu", [P, 2, S], F32))
        qk, _, v_tok, r_act, zk, state, kend_tok, sc, tmp, stat = overlay(
            ("qk", [P, HEADS, 2, S], F32), ("gap0", [P, KT, S], F32),
            ("v_tok", [P, PAIRS, DV], F32), ("r_act", [P, KT, S], F32), ("zk", [P, HEADS, S], F32),
            ("state", [P, N_CHUNK, HV], F32), ("kend_tok", [P, PAIRS, P], F32), ("sc", [P, S], F32),
            ("tmp", [P, 5, S], F32), ("stat", [P, S], F32))
        o_hi, o_lo = overlay(("o_hi", [P, KT, S], F32R), ("o_lo", [P, KT, S], F32R))
        _, u_p, p_hi, p_lo = overlay(
            ("gap1", [P, 2 * KT, S], F32), ("u_p", [P, POOL_GROUPS, S], F32),
            ("p_hi", [P, POOL_GROUPS, S], F32R), ("p_lo", [P, POOL_GROUPS, S], F32R))
        _, m_hi, m_lo, pooled_hi, pooled_lo, sg, sp_ = overlay(
            ("gap3", [P, 2 * KT, S], F32), ("m_hi", [P, KT, S], F32R), ("m_lo", [P, KT, S], F32R),
            ("pooled_hi", [P, POOL_GROUPS, S], F32R), ("pooled_lo", [P, POOL_GROUPS, S], F32R),
            ("sg", [P, TILE_N, S], F32), ("sp_", [P, TILE_N, S], F32))
        _, win, a_sb = overlay(("gap2", [P, 44, S], F32), ("win", [P, 2, S], F32), ("a_sb", [RANK, S], F32))
        sb("arena", [P, 48, S])

        bank = [ctx.enter_context(nc.psum_tensor(f"bank{i}", [P, S], F32)) for i in range(8)]
        B_OUT, B_KV, B_T, B_ADA = bank[4], bank[5], bank[6], bank[7]

        in_x = sem("in_x")
        in_small = sem("in_small")
        in_ada = [sem(f"in_ada{i}") for i in range(4)]
        in_alpha = sem("in_alpha")
        landed = [[sem(f"landed{i}{j}") for j in range(2)] for i in range(2)]
        w_hi = sem("w_hi")
        w_lo = sem("w_lo")
        quarter = sem("quarter")
        bank_read = [sem(f"bank_read{i}") for i in range(TILE_N)]
        consts = sem("consts")
        c_ready = sem("c_ready")
        small_t = sem("small_t")
        small_r = sem("small_r")
        x_t = sem("x_t")
        x_r = sem("x_r")
        ada0 = sem("ada0")
        first_h, first_hi = sem("first_h"), sem("first_hi")
        h_ready = sem("h_ready")
        ada_in = [sem("ada_in0"), sem("ada_in1")]
        ada_step = sem("ada_step")
        ada_red = sem("ada_red")
        coef = sem("coef")
        act_hi_done = sem("act_hi_done")
        act_ready = sem("act_ready")
        ln_zero = sem("ln_zero")
        ln_sqd = sem("ln_sqd")
        ln_sum = sem("ln_sum")
        ln_pe, ln_act, ln_dve = sem("ln_pe"), sem("ln_act"), sem("ln_dve")
        a_act = sem("a_act")
        layer_copied = sem("layer_copied")
        z_pe = sem("z_pe")
        sc_zero = sem("sc_zero")
        prep_dve, prep_act = sem("prep_dve"), sem("prep_act")
        state_pe, state_dve = sem("state_pe"), sem("state_dve")
        kend_read = sem("kend_read")
        out_pe, norm_act, norm_dve = sem("out_pe"), sem("norm_act"), sem("norm_dve")
        o_hi_done = sem("o_hi_done")
        win_dve = sem("win_dve")
        p_hi_done, p_ready = sem("p_hi_done"), sem("p_ready")
        pooled_hi_done, pooled_ready = sem("pooled_hi_done"), sem("pooled_ready")
        merged, m_hi_done, m_ready = sem("merged"), sem("m_hi_done"), sem("m_ready")
        out_t, out_r, stored = sem("out_t"), sem("out_r"), sem("stored")

        def block_no(l, nb, g=0, per=0):
            return l * NB + g * per + nb

        def split_done(l, nb, g=0, per=0):
            return block_no(l, nb, g, per) + 3

        def quarters(l, nb, f, g=0, per=0):
            return l * (4 * NB) + g * (4 * per) + 4 * nb + f + 1 + 8

        def landings(l, nb, g=0, per=0):
            return l * (8 * NB) + g * (8 * per) + 16 * (nb // 2 + 1)

        def free_for(l, group, g=0):
            return l * NG + g + group + 1

        def read_in(l, group, g=0):
            return free_for(l, group, g) + 1

        def tile(t, i):
            if isinstance(i, int):
                return t[:, i, :]
            return t[:, bass.ds(i, 1), :].rearrange("p a s -> p (a s)")

        P_LAYER = 2 * DEPTH * 3 * KT
        PER_LAYER = KT + 2 * POOL_GROUPS

        up = [ffn1_up.rearrange("l (k p) (h n) -> l p k h n", p=P, h=2), None,
              ffn2_up.rearrange("l (k p) (h n) -> l p k h n", p=P, h=2)]
        down = [ffn1_down.rearrange("l (k p) n -> l p k n", p=P), None,
                ffn2_down.rearrange("l (k p) n -> l p k n", p=P)]
        win_v = w_in.rearrange("l (k p) n -> l p k n", p=P)
        pg_v = w_proj_gla.rearrange("l (k p) n -> l p k n", p=P)
        pp_v = w_proj_pool.rearrange("l (k p) n -> l p k n", p=P)
        wo_v = w_out.rearrange("l (k p) n -> l p k n", p=P)
        wpool_v = w_pool.rearrange("l g i o -> l i g o")
        ada_v = w_ada.rearrange("l (k p) n -> l p k n", p=P)

        block = ctx.enter_context(nc.Block())

        @block.sync
        def _(sp):
            for t in range(PAIRS):
                sp.dma_start(x_tok[:, t, :], x[0, t * P:(t + 1) * P, :]).then_inc(in_x, 16)
            for i in range(4):
                sp.dma_start(ada_start[:, i, :, :], ada_v[0, :, :, i * 512:(i + 1) * 512]).then_inc(in_ada[i], 16)

            def load(src, l, nb, size, g=0, per=0, width=512):
                sp.wait_ge(w_lo, block_no(l, nb, g, per) + 1)
                slot = nb % 2
                for i in range(2):
                    if width == "gate/up":
                        dst = raw[:, slot, 0:size].rearrange("p (k h n) -> p k h n", h=2, n=2 * P)[:, :, i, :]
                        part = src[:, :, i, :]
                    else:
                        dst = raw[:, slot, i * size // 2:(i + 1) * size // 2].rearrange("p (k n) -> p k n", n=width)
                        ks = size // width
                        part = src[:, i * ks // 2:(i + 1) * ks // 2, :]
                    sp.dma_start(dst, part).then_inc(landed[slot][i], 16)

            def load_ffn(l, s):
                base = STAGE_BLOCKS * s
                with sp.Fori(0, UP_GROUPS) as g:
                    for b in range(UP_BLOCKS):
                        load(up[s][l, :, 4 * b:4 * b + 4, :, bass.ds(g * (2 * P), 2 * P)], l, base + b, SLOT,
                             g, UP_BLOCKS, width="gate/up")
                with sp.Fori(0, DOWN_GROUPS) as g:
                    k0 = 0
                    for b, ks in enumerate(DOWN_KS):
                        load(down[s][l, :, k0:k0 + ks, bass.ds(g * 512, 512)], l, base + DOWN0 + b,
                             ks * 512, g, DOWN_BLOCKS)
                        k0 += ks

            def load_mix(l):
                sp.wait_ge(z_pe, l * HEADS + HEADS)
                sp.dma_start(alpha_w[:, :], w_alpha[l]).then_inc(in_alpha, 16)
                nb = STAGE_BLOCKS
                for name, n, size, _ in MIX:
                    for b in range(n):
                        ks = slice(4 * b, 4 * b + 4)
                        half = int(name[-1]) * 512 if name[-1].isdigit() else 0
                        if name == "a":
                            src, w = win_v[l, :, :, COL_A:COL_A + RANK], RANK
                        elif name == "wp":
                            src, w = wpool_v[l], P
                        elif name[:2] == "yg":
                            src, w = pg_v[l, :, ks, half:half + 512], 512
                        elif name[:2] == "yp":
                            src, w = pp_v[l, :, :, half:half + 512], 512
                        elif name[:3] == "out":
                            src, w = wo_v[l, :, ks, half:half + 512], 512
                        else:
                            col = {"q": COL_Q, "k": COL_K, "v": COL_V, "r": COL_R, "u": COL_U,
                                   "gg": COL_GG, "gp": COL_GP}[name.rstrip("01")] + half
                            src, w = win_v[l, :, ks, col:col + 512], 512
                        load(src, l, nb, size, width=w)
                        nb += 1

            with sp.Fori(0, DEPTH) as l:
                load_ffn(l, 0)
                load_mix(l)
                load_ffn(l, 2)
            for b in range(2):
                load(wo_v[0, :, 0:4, 0:512], DEPTH, b, SLOT)
            sp.wait_ge(out_r, KT)
            for t in range(PAIRS):
                sp.dma_start(out[0, t * P:(t + 1) * P, :], out_tok[:, t, :]).then_inc(stored, 16)
            sp.wait_ge(stored, 16 * PAIRS)

        @block.gpsimd
        def _(pool):
            row = 0
            srcs = [ln_g.rearrange("l s (t p) -> (l s t) p", p=P), ln_b.rearrange("l s (t p) -> (l s t) p", p=P)]
            for l in range(DEPTH):
                srcs += [gla_norm_g[l].rearrange("h (t p) -> (h t) p", p=P),
                         pool_scale[l].rearrange("(t p) -> t p", p=P), b_alpha[l].rearrange("(t p) -> t p", p=P)]
            for src in srcs:
                n = src.shape[0]
                pool.dma_start(stage_rows[row:row + n, 0, :], src).then_inc(in_small, 16)
                row += n
            rows = N_MOD * KT
            for l in range(DEPTH):
                pool.dma_start(stage_rows[0:rows, 1 + l, :],
                               b_ada[l].rearrange("(t p) -> t p", p=P)).then_inc(in_small, 16)
            pool.dma_start(stage_rows[rows:rows + KT, 1, :], c.rearrange("a (t p) -> (a t) p", p=P)).then_inc(in_small, 16)
            nc.gpsimd.memset(ones[:, :], 1.0).then_inc(consts, 1)
            nc.gpsimd.memset(ident[:, :], 0.0).then_inc(consts, 1)
            for i in range(WINDOWS[-1]):
                last = nc.gpsimd.memset(cinv[:, i:i + 1], 1.0 / (i + 1))
            last.then_inc(consts, 1)
            pool.wait_ge(consts, 3)
            nc.gpsimd.affine_select(out=ident[:, :], in_=ident[:, :], compare_op=ALU.not_equal, fill=1.0,
                                    base=0, pattern=[[-1, P]], channel_multiplier=1).then_inc(consts, 1)
            nc.gpsimd.affine_select(out=maskf[:, :], in_=ones[:, :], compare_op=ALU.is_ge, fill=0.0,
                                    base=0, pattern=[[1, P]], channel_multiplier=-1).then_inc(consts, 1)
            pool.wait_ge(consts, 5)
            nc.gpsimd.memset(maskf[0:CHUNK, CHUNK:P], 0.0).then_inc(consts, 1)
            pool.wait_ge(consts, 6)
            nc.gpsimd.tensor_copy(mask[:, :], maskf[:, :]).then_inc(consts, 1)

            pool.wait_ge(c_ready, 1)

            def columns(src_l, col0, g, first, per_layer, l):
                for i in range(2):
                    pool.wait_ge(ada_red, l * per_layer + g * 2 + (first + i) + 1)
                    pool.dma_start(ada[:, i, :, :], ada_v[src_l, :, :, bass.ds(g * (2 * P) + (col0 + i * P), P)])\
                        .then_inc(ada_in[i], 16)
                for i in range(2):
                    done = l * (4 * per_layer) + g * 8 + 4 * (first + i)
                    pool.wait_ge(ada_in[i], l * (8 * per_layer) + g * 16 + 8 * first + 16)
                    nc.gpsimd.tensor_tensor(ada[:, i, :, :], ada[:, i, :, :],
                                            c_act[:, :].unsqueeze(2).to_broadcast([P, KT, P]), ALU.mult)\
                        .then_inc(ada_step, 1)
                    for n, w in enumerate((KT // 2, KT // 4, KT // 8)):
                        pool.wait_ge(ada_step, done + n + 1)
                        nc.gpsimd.tensor_tensor(ada[:, i, 0:w, :], ada[:, i, 0:w, :], ada[:, i, w:2 * w, :],
                                                ALU.add).then_inc(ada_step, 1)

            here = (N_MOD - 2) * KT
            with pool.Fori(0, DEPTH) as l:
                with pool.Fori(0, here // 2) as g:
                    columns(l, 2 * D, g, 0, 3 * ADA, l)
                with pool.Fori(0, KT) as g:
                    columns((l + 1) % DEPTH, 0, g, here, 3 * ADA, l)

        @block.scalar
        def _(act):
            for f in range(TILE_N):
                act.sem_inc(bank_read[f], 1)
            copy = nc.scalar.copy

            def split_hi(l, nb, size, g=0, per=0):
                slot = nb % 2
                for half in range(2):
                    act.wait_ge(landed[slot][half], landings(l, nb, g, per))
                act.wait_ge(quarter, quarters(l, nb - 2, TILE_N - 1, g, per))
                copy(wh[:, slot, 0:size], raw[:, slot, 0:size]).then_inc(w_hi, 1)

            def touch_table(func):
                nc.scalar.activation(touch[:, :], ones[:, 0:1], func)

            act.wait_ge(small_t, 1)
            copy(params[:, :], bank[4][:, 0:P]).then_inc(small_r, 1)
            act.wait_ge(small_t, 2)
            copy(bias[:, 0:N_MOD * KT], bank[5][:, 0:N_MOD * KT]).then_inc(small_r, 1)
            nc.scalar.activation(c_act[:, :], bank[5][:, N_MOD * KT:N_MOD * KT + KT], ACT.Silu).then_inc(c_ready, 1)
            act.wait_ge(small_t, 3)
            copy(bias[:, N_MOD * KT:2 * N_MOD * KT], bank[6][:, 0:N_MOD * KT]).then_inc(small_r, 1)
            for t in range(KT):
                act.wait_ge(x_t, t + 1)
                copy(xT[:, t, :], bank[t % TILE_N][:, :]).then_inc(x_r, 1)
            split_hi(0, 0, SLOT)
            split_hi(0, 1, SLOT)
            for t in range(KT):
                act.wait_ge(first_h, t + 1)
                copy(h_hi[:, t, :], ln_h[:, t % 2, :]).then_inc(first_hi, 1)

            def squares(l, s, group, g=0):
                for f in range(TILE_N):
                    act.wait_ge(bank_read[f], read_in(l, group, g))
                    act.wait_ge(ln_sum, l * (6 * KT) + g * (2 * TILE_N) + 2 * (s * KT + f) + 2)
                    nc.scalar.activation(ln_sq[:, f % 2, :], tile(xT, g * TILE_N + f), ACT.Square)\
                        .then_inc(ln_sqd, 1)

            def layer_norm(l, s):
                turn = l * 3 + s
                touch_table(ACT.Sqrt)
                split_hi(l, STAGE_BLOCKS * (s + 1) + 1, SLOT)
                act.wait_ge(ln_pe, at(turn, LN_PE, "sum"))
                nc.scalar.activation(ln_tmp[:, :], B_OUT[:, :], ACT.Square, scale=1.0 / D).then_inc(ln_act, 1)
                nc.scalar.activation(mean[:, :], B_OUT[:, :], ACT.Copy, scale=1.0 / D).then_inc(ln_act, 1)
                act.wait_ge(ln_dve, at(turn, LN_DVE, "veps"))
                nc.scalar.activation(rstd[:, :], rstd[:, :], ACT.Sqrt).then_inc(ln_act, 1)
                touch_table(ACT.Silu)
                for t in range(KT):
                    act.wait_ge(ln_dve, at(turn, LN_DVE, f"h{t}"))
                    copy(h_hi[:, t, :], ln_h[:, t % 2, :]).then_inc(ln_act, 1)
                    nc.scalar.activation(xT[:, t, :], ln_n[:, t % 2, :], ACT.Identity,
                                         bias=lb[:, t:t + 1], scale=lg[:, t:t + 1]).then_inc(ln_act, 1)
                act.wait_ge(ln_act, at(turn, LN_ACT, f"x{KT - 1}"))

            def hidden(l, s, g):
                group, last = GROUP0[s], STAGE_BLOCKS * s + 1
                for i in range(2):
                    f = 2 * i
                    n = l * (2 * FT) + (s // 2) * FT + 2 * g + i
                    act.wait_ge(quarter, quarters(l, last, f, g, UP_BLOCKS))
                    act.wait_ge(act_ready, n + 1)
                    nc.scalar.activation(silu[:, i, :], bank[f][:, :], ACT.Silu).then_inc(bank_read[f], 1)
                    act.wait_ge(bank_read[f + 1], read_in(l, group, g))
                    copy(tile(act_hi, 2 * g + i), silu[:, i, :]).then_inc(act_hi_done, 1)

            def ffn(l, s):
                base = STAGE_BLOCKS * s
                split_hi(l, base + 2, SLOT)
                hidden(l, s, 0)
                with act.Fori(1, UP_GROUPS) as g:
                    split_hi(l, base + 1, SLOT, g, UP_BLOCKS)
                    split_hi(l, base + 2, SLOT, g, UP_BLOCKS)
                    hidden(l, s, g)
                with act.Fori(0, DOWN_GROUPS) as g:
                    for b in range(DOWN_BLOCKS):
                        size = DOWN_KS[(b + 1) % DOWN_BLOCKS] * 512
                        split_hi(l, base + DOWN0 + b + 1, size, g, DOWN_BLOCKS)
                    squares(l, s, GROUP0[s] + UP_GROUPS, g)
                layer_norm(l, s)

            def prepare(l, h):
                turn = l * HEADS + h
                act.wait_ge(prep_dve, at(turn, PREP_DVE, "nabs"))
                nc.scalar.activation(tmp[:, 0, :], tmp[:, 0, :], ACT.Exp).then_inc(prep_act, 1)
                act.wait_ge(prep_act, at(turn, PREP_ACT, "exp"))
                nc.scalar.activation(tmp[:, 0, :], tmp[:, 0, :], ACT.Ln, bias=1.0).then_inc(prep_act, 1)
                act.wait_ge(prep_dve, at(turn, PREP_DVE, "b"))
                nc.scalar.activation(tmp[:, 0, :], zk[:, h, :], ACT.Exp, scale=1.0 / TAU).then_inc(prep_act, 1)
                nc.scalar.activation(tmp[:, 1, :], zk[:, h, :], ACT.Exp, scale=-1.0 / TAU).then_inc(prep_act, 1)
                act.wait_ge(prep_dve, at(turn, PREP_DVE, "to_end"))
                nc.scalar.activation(tmp[:, 2, :], tmp[:, 2, :], ACT.Exp, scale=1.0 / TAU).then_inc(prep_act, 1)

            def high_of_output(l, h):
                turn = l * HEADS + h
                for d in range(2):
                    act.wait_ge(norm_dve, at(turn, NORM_DVE, f"g{d}"))
                    copy(o_hi[:, 2 * h + d, :], tmp[:, 2 * (h % 2) + d, :]).then_inc(o_hi_done, 1)

            def attend(l, i):
                for what, h in gla_slot(i):
                    turn = l * HEADS + h
                    out0 = 2 * (h % 2)
                    if what == "kT":
                        act.wait_ge(state_pe, at(turn, STATE_PE, "kT"))
                        copy(kend_tok[:, :, :], B_T[:, :].rearrange("p (a d) -> p a d", d=P)).then_inc(kend_read, 1)
                    elif what == "o0":
                        act.wait_ge(out_pe, at(turn, OUT_PE, "o0"))
                        if h >= 2:
                            act.wait_ge(norm_dve, at(turn - 2, NORM_DVE, "lo1"))
                        copy(tmp[:, out0, :], B_OUT[:, :]).then_inc(norm_act, 1)
                        if h:
                            high_of_output(l, h - 1)
                    elif what == "o1":
                        act.wait_ge(out_pe, at(turn, OUT_PE, "o1"))
                        copy(tmp[:, out0 + 1, :], B_OUT[:, :]).then_inc(norm_act, 1)
                        if h:
                            act.wait_ge(norm_dve, at(turn - 1, NORM_DVE, "n1"))
                        act.wait_ge(norm_act, at(turn, NORM_ACT, "o1"))
                        nc.scalar.activation(tmp[:, 4, :], tmp[:, out0, :], ACT.Square).then_inc(norm_act, 1)
                        nc.scalar.activation(stat[:, :], tmp[:, out0 + 1, :], ACT.Square).then_inc(norm_act, 1)
                    elif what == "stats":
                        act.wait_ge(out_pe, at(turn, OUT_PE, "sq"))
                        nc.scalar.activation(zk[:, h, :], B_OUT[:, :], ACT.Copy, scale=1.0 / HV).then_inc(norm_act, 1)
                        nc.scalar.activation(stat[:, :], B_OUT[:, :], ACT.Square, scale=1.0 / HV).then_inc(norm_act, 1)
                        act.wait_ge(norm_dve, at(turn, NORM_DVE, "veps"))
                        nc.scalar.activation(tmp[:, 4, :], tmp[:, 4, :], ACT.Sqrt).then_inc(norm_act, 1)
                        if h == HEADS - 1:
                            high_of_output(l, h)

            def mixer(l):
                nb = STAGE_BLOCKS
                for name, n, size, _ in MIX:
                    half = int(name[-1]) if name[-1].isdigit() else 0
                    group = GROUP0[1] + MIX_GROUP[name]
                    for b in range(n):
                        j = nb - STAGE_BLOCKS
                        if j > 0:
                            split_hi(l, nb + 1, MIX_SIZE[j + 1])
                        nb += 1
                        last = b == n - 1
                        if name[0] == "v":
                            prepare(l, 2 * half + b)
                        if name == "gg0" and last:
                            act.wait_ge(norm_dve, at(l * HEADS + HEADS - 1, NORM_DVE, "lo1"))
                        if name in ("gg1", "gp1") and last:
                            act.wait_ge(merged, l * KT + TILE_N)
                        for f in range(TILE_N):
                            if last and name not in ("a", "wp", "yg0", "yg1", "yp0", "yp1", "out0", "out1"):
                                act.wait_ge(quarter, quarters(l, nb - 1, f))
                                kind = name.rstrip("01")
                                if kind == "q":
                                    ins = copy(qk[:, f, 0, :], bank[f][:, :])
                                elif kind == "k":
                                    ins = copy(qk[:, f, 1, :], bank[f][:, :])
                                elif kind == "v":
                                    ins = copy(v_tok[:, f, half * 512:half * 512 + 512], bank[f][:, :])
                                elif kind == "r":
                                    ins = nc.scalar.activation(r_act[:, TILE_N * half + f, :], bank[f][:, :], ACT.Silu)
                                elif kind == "u":
                                    ins = copy(u_p[:, f, :], bank[f][:, :])
                                else:
                                    dst = sg if kind == "gg" else sp_
                                    ins = nc.scalar.activation(dst[:, f, :], bank[f][:, :], ACT.Sigmoid)
                                ins.then_inc(bank_read[f], 1)
                            if name in GLA_GROUPS:
                                attend(l, GLA_GROUPS[name] + TILE_N * b + f)
                        if name == "a":
                            act.wait_ge(quarter, quarters(l, nb - 1, TILE_N - 1))
                            copy(a_sb[:, :], B_T[0:RANK, :]).then_inc(a_act, 1)
                        if name == "gg0" and last:
                            for g in range(POOL_GROUPS):
                                act.wait_ge(win_dve, l * WINDOW_STEPS + sum(2 * (i + 1) + 3 for i in range(g + 1)))
                                copy(p_hi[:, g, :], u_p[:, g, :]).then_inc(p_hi_done, 1)
                        if name == "wp":
                            for f in range(TILE_N):
                                act.wait_ge(bank_read[f], read_in(l, group))
                                copy(pooled_hi[:, f, :], u_p[:, f, :]).then_inc(pooled_hi_done, 1)
                        if name[:2] == "yp":
                            for f in range(TILE_N):
                                act.wait_ge(merged, l * KT + TILE_N * half + f + 1)
                                copy(m_hi[:, TILE_N * half + f, :], sp_[:, f, :]).then_inc(m_hi_done, 1)
                        if name[:3] == "out" and last:
                            squares(l, 1, GROUP0[1] + MIX_GROUP["out0"], half)
                layer_norm(l, 1)

            with act.Fori(0, DEPTH) as l:
                ffn(l, 0)
                mixer(l)
                ffn(l, 2)
            for t in range(KT):
                act.wait_ge(out_t, t + 1)
                copy(out_tok[:, :, t * P:(t + 1) * P], bank[t % TILE_N][:, :].rearrange("p (a d) -> p a d", d=P))\
                    .then_inc(out_r, 1)

        @block.vector
        def _(dve):
            v = nc.vector
            dve.sem_inc(w_lo, 2)
            dve.sem_inc(act_ready, 2)
            dve.sem_inc(ln_sum, 4)

            def split_lo(l, nb, size, g=0, per=0):
                slot = nb % 2
                dve.wait_ge(w_hi, block_no(l, nb, g, per) + 1)
                v.tensor_tensor(wl[:, slot, 0:size], raw[:, slot, 0:size], wh[:, slot, 0:size].bitcast(F32),
                                ALU.subtract).then_inc(w_lo, 1)

            dve.wait_ge(small_r, 3)
            dve.wait_ge(consts, 7)
            dve.wait_ge(ada0, 1)
            v.memset(bias[:, 2 * N_MOD * KT:], 0.0)
            v.tensor_tensor(mods[:, KT:ADA], B_ADA[:, KT:ADA], bias[:, 0:2 * KT], ALU.add).then_inc(coef, 1)
            dve.wait_ge(coef, 1)
            v.tensor_scalar(scale1[:, :], mods[:, 2 * KT:ADA], 1.0, None, ALU.add).then_inc(coef, 1)
            dve.wait_ge(coef, 2)
            dve.sem_inc(coef, len(COEF) - 2)
            dve.wait_ge(x_r, KT)
            for t in range(KT):
                v.tensor_scalar(ln_h[:, t % 2, :], xT[:, t, :], scale1[:, t:t + 1], mods[:, KT + t:KT + t + 1],
                                ALU.mult, ALU.add).then_inc(first_h, 1)
                dve.wait_ge(first_hi, t + 1)
                v.tensor_tensor(h_lo[:, t, :], ln_h[:, t % 2, :], h_hi[:, t, :].bitcast(F32),
                                ALU.subtract).then_inc(h_ready, 1)
                if t == 0:
                    split_lo(0, 0, SLOT)
                if t == 4:
                    split_lo(0, 1, SLOT)

            def coefficients(l, s):
                turn = l * 3 + s
                half = 1.0 if s == 1 else 0.5
                dve.wait_ge(ada_red, (turn + 1) * ADA + 2)

                def done(name):
                    return at(turn + 1, COEF, name)
                v.tensor_tensor(mods[:, :], B_ADA[:, 0:ADA],
                                bias[:, bass.ds(l * (N_MOD * KT) + (3 * s + 2) * KT, ADA)], ALU.add).then_inc(coef, 1)
                dve.wait_ge(coef, done("mods"))
                v.tensor_scalar(gate[:, :], mods[:, 0:KT], 1.0, half / ALPHA, ALU.add, ALU.mult).then_inc(coef, 1)
                v.tensor_scalar(scale1[:, :], mods[:, 2 * KT:ADA], 1.0, None, ALU.add).then_inc(coef, 1)
                dve.wait_ge(coef, done("scale1"))
                ln_gain = params[:, bass.ds(l * (3 * KT) + s * KT, KT)]
                ln_bias = params[:, bass.ds(l * (3 * KT) + (DEPTH * 3 + s) * KT, KT)]
                v.tensor_tensor(gs[:, :], scale1[:, :], ln_gain, ALU.mult).then_inc(coef, 1)
                v.tensor_tensor(bs[:, :], scale1[:, :], ln_bias, ALU.mult).then_inc(coef, 1)
                dve.wait_ge(coef, done("bs1"))
                v.tensor_tensor(bs[:, :], bs[:, :], mods[:, KT:2 * KT], ALU.add).then_inc(coef, 1)
                v.tensor_copy(lg[:, :], ln_gain).then_inc(coef, 1)
                v.tensor_copy(lb[:, :], ln_bias).then_inc(coef, 1)

            def clear_sums(l, s):
                v.memset(ln_acc[:, :], 0.0).then_inc(ln_zero, 1)
                v.memset(ln_accq[:, :], 0.0).then_inc(ln_zero, 1)
                dve.wait_ge(ln_zero, (l * 3 + s) * 2 + 2)

            def residual(l, s, group, last, g=0, per=0):
                for f in range(TILE_N):
                    n = l * (6 * KT) + g * (2 * TILE_N) + 2 * (s * KT + f) + 4
                    t = g * TILE_N + f
                    dve.wait_ge(quarter, quarters(l, last, f, g, per))
                    v.scalar_tensor_tensor(out=tile(xT, t), in0=bank[f][:, :],
                                           scalar=gate[:, bass.ds(t, 1)], in1=tile(xT, t),
                                           op0=ALU.mult, op1=ALU.add).then_inc(bank_read[f], 1)
                    dve.wait_ge(bank_read[f], read_in(l, group, g))
                    dve.wait_ge(ln_sum, n)
                    v.tensor_tensor(ln_acc[:, :], ln_acc[:, :], tile(xT, t), ALU.add).then_inc(ln_sum, 1)
                    dve.wait_ge(ln_sqd, l * (3 * KT) + g * TILE_N + s * KT + f + 1)
                    v.tensor_tensor(ln_accq[:, :], ln_accq[:, :], ln_sq[:, f % 2, :], ALU.add).then_inc(ln_sum, 1)

            def layer_norm(l, s):
                turn = l * 3 + s

                def low(t):
                    dve.wait_ge(ln_act, at(turn, LN_ACT, f"hi{t}"))
                    v.tensor_tensor(h_lo[:, t, :], ln_h[:, t % 2, :], h_hi[:, t, :].bitcast(F32),
                                    ALU.subtract).then_inc(h_ready, 1)

                def centre(t):
                    if t >= 2:
                        dve.wait_ge(ln_act, at(turn, LN_ACT, f"x{t - 2}"))
                    v.tensor_tensor(ln_n[:, t % 2, :], xT[:, t, :], mean[:, :], ALU.subtract).then_inc(ln_dve, 1)

                def scaled(t):
                    dve.wait_ge(ln_dve, at(turn, LN_DVE, "rec" if t == 0 else f"c{t}"))
                    v.tensor_tensor(ln_n[:, t % 2, :], ln_n[:, t % 2, :], rstd[:, :], ALU.mult).then_inc(ln_dve, 1)
                    dve.wait_ge(ln_dve, at(turn, LN_DVE, f"n{t}"))
                    v.tensor_scalar(ln_h[:, t % 2, :], ln_n[:, t % 2, :], gs[:, t:t + 1], bs[:, t:t + 1],
                                    ALU.mult, ALU.add).then_inc(ln_dve, 1)

                dve.wait_ge(coef, at(turn + 1, COEF, "lb"))
                dve.wait_ge(ln_pe, at(turn, LN_PE, "sq"))
                dve.wait_ge(ln_act, at(turn, LN_ACT, "msq"))
                v.scalar_tensor_tensor(out=rstd[:, :], in0=B_KV[:, :], scalar=1.0 / D, in1=ln_tmp[:, :],
                                       op0=ALU.mult, op1=ALU.subtract).then_inc(ln_dve, 1)
                dve.wait_ge(ln_dve, at(turn, LN_DVE, "var"))
                v.tensor_scalar(rstd[:, :], rstd[:, :], 0.0, LN_EPS / ALPHA ** 2, ALU.max, ALU.add).then_inc(ln_dve, 1)
                dve.wait_ge(ln_act, at(turn, LN_ACT, "mean"))
                centre(0)
                dve.wait_ge(ln_act, at(turn, LN_ACT, "sqrt"))
                v.reciprocal(rstd[:, :], rstd[:, :]).then_inc(ln_dve, 1)
                scaled(0)
                for t in range(1, KT):
                    centre(t)
                    low(t - 1)
                    scaled(t)
                    if t == 4:
                        split_lo(l, STAGE_BLOCKS * (s + 1) + 1, SLOT)
                low(KT - 1)

            def hidden(l, s, g):
                group, last = GROUP0[s], STAGE_BLOCKS * s + 1
                for i in range(2):
                    f = 2 * i + 1
                    n = l * (2 * FT) + (s // 2) * FT + 2 * g + i
                    dve.wait_ge(quarter, quarters(l, last, f, g, UP_BLOCKS))
                    dve.wait_ge(bank_read[f - 1], read_in(l, group, g))
                    v.tensor_tensor(silu[:, i, :], silu[:, i, :], bank[f][:, :], ALU.mult).then_inc(bank_read[f], 1)
                    dve.wait_ge(act_hi_done, n + 1)
                    v.tensor_tensor(tile(act_lo, 2 * g + i), silu[:, i, :], tile(act_hi, 2 * g + i).bitcast(F32),
                                    ALU.subtract).then_inc(act_ready, 1)

            def ffn(l, s):
                base = STAGE_BLOCKS * s
                split_lo(l, base + 2, SLOT)
                hidden(l, s, 0)
                with dve.Fori(1, UP_GROUPS) as g:
                    split_lo(l, base + 1, SLOT, g, UP_BLOCKS)
                    split_lo(l, base + 2, SLOT, g, UP_BLOCKS)
                    hidden(l, s, g)
                dve.wait_ge(quarter, quarters(l, base + DOWN0 - 1, TILE_N - 1))
                clear_sums(l, s)
                coefficients(l, s)
                with dve.Fori(0, DOWN_GROUPS) as g:
                    for b in range(DOWN_BLOCKS):
                        size = DOWN_KS[(b + 1) % DOWN_BLOCKS] * 512
                        split_lo(l, base + DOWN0 + b + 1, size, g, DOWN_BLOCKS)
                    residual(l, s, GROUP0[s] + UP_GROUPS, base + DOWN0 + DOWN_BLOCKS - 1, g, DOWN_BLOCKS)
                layer_norm(l, s)

            def prepare(l, h):
                turn = l * HEADS + h
                t0, t1, t2 = tmp[:, 0, :], tmp[:, 1, :], tmp[:, 2, :]
                q, k, b = qk[:, h, 0, :], qk[:, h, 1, :], zk[:, h, :]

                def step(ins):
                    ins.then_inc(prep_dve, 1)

                def wait(sem_, steps, name):
                    dve.wait_ge(sem_, at(turn, steps, name))
                step(v.tensor_scalar(t1, b, 0.0, None, ALU.min))
                wait(prep_dve, PREP_DVE, "min")
                step(v.scalar_tensor_tensor(out=t0, in0=t1, scalar=2.0, in1=b, op0=ALU.mult, op1=ALU.subtract))
                wait(prep_act, PREP_ACT, "ln")
                step(v.tensor_tensor(t1, t1, t0, ALU.subtract))
                wait(prep_dve, PREP_DVE, "log_a")
                for n in range(N_CHUNK):
                    cols = slice(n * CHUNK, (n + 1) * CHUNK)
                    ins = v.tensor_tensor_scan(zk[:, h, cols], ones[:, 0:CHUNK], tmp[:, 1, cols], 0.0, ALU.mult, ALU.add)
                step(ins)
                wait(prep_dve, PREP_DVE, "b")
                b3 = b.rearrange("p (n c) -> p n c", c=CHUNK)
                step(v.tensor_tensor(t2.rearrange("p (n c) -> p n c", c=CHUNK),
                                     b3[:, :, CHUNK - 1:CHUNK].to_broadcast([P, N_CHUNK, CHUNK]), b3, ALU.subtract))
                wait(prep_act, PREP_ACT, "exp_end")
                step(v.tensor_tensor(b, k, t2, ALU.mult))
                step(v.scalar_tensor_tensor(out=q, in0=q, scalar=float(DK // HEADS) ** -0.5, in1=t0,
                                            op0=ALU.mult, op1=ALU.mult))
                step(v.tensor_copy(decay[:, h, :], tmp[:, 0, CHUNK - 1::CHUNK]))
                step(v.tensor_tensor(k, k, t1, ALU.mult))
                wait(prep_dve, PREP_DVE, "kt")

            def normalise(l, h):
                turn = l * HEADS + h
                sd = tmp[:, 4, :]
                dve.wait_ge(norm_act, at(turn, NORM_ACT, "sqrt"))
                v.reciprocal(sd, sd).then_inc(norm_dve, 1)
                for d in range(2):
                    o = tmp[:, 2 * (h % 2) + d, :]
                    t = 2 * h + d
                    if d == 0:
                        dve.wait_ge(norm_dve, at(turn, NORM_DVE, "rec"))
                    v.tensor_tensor(o, o, zk[:, h, :], ALU.subtract).then_inc(norm_dve, 1)
                    dve.wait_ge(norm_dve, at(turn, NORM_DVE, f"c{d}"))
                    v.tensor_tensor(o, o, sd, ALU.mult).then_inc(norm_dve, 1)
                    dve.wait_ge(norm_dve, at(turn, NORM_DVE, f"n{d}"))
                    dve.wait_ge(bank_read[t % TILE_N], read_in(l, GROUP0[1] + MIX_GROUP[f"r{t // TILE_N}"]))
                    v.scalar_tensor_tensor(out=o, in0=o, scalar=layer_p[:, t:t + 1], in1=r_act[:, t, :],
                                           op0=ALU.mult, op1=ALU.mult).then_inc(norm_dve, 1)
                for d in range(2):
                    t = 2 * h + d
                    dve.wait_ge(o_hi_done, l * KT + t + 1)
                    v.tensor_tensor(o_lo[:, t, :], tmp[:, 2 * (h % 2) + d, :], o_hi[:, t, :].bitcast(F32),
                                    ALU.subtract).then_inc(norm_dve, 1)

            def attend(l, i):
                for what, h in gla_slot(i):
                    turn = l * HEADS + h
                    if what == "sc":
                        dve.wait_ge(state_pe, at(turn, STATE_PE, "sc"))
                        v.memset(touch_v[:, :], 0.0)
                        v.copy_predicated(sc[:, :].rearrange("p (a d) -> p a d", d=P),
                                          mask[:, :].unsqueeze(1).to_broadcast([P, PAIRS, P]),
                                          B_T[:, :].rearrange("p (a d) -> p a d", d=P)).then_inc(state_dve, 1)
                    elif what[:2] == "kv":
                        dve.wait_ge(state_pe, at(turn, STATE_PE, what))
                        n = int(what[2])
                        new = (B_KV, B_T)[n % 2][:, 0:HV]
                        if n == 0:
                            ins = v.tensor_copy(state[:, 1, :], new)
                        else:
                            dve.wait_ge(state_dve, at(turn, STATE_DVE, f"S{n}"))
                            ins = v.scalar_tensor_tensor(out=state[:, n + 1, :], in0=state[:, n, :],
                                                         scalar=decay[:, h, n:n + 1], in1=new,
                                                         op0=ALU.mult, op1=ALU.add)
                        ins.then_inc(state_dve, 1)
                    elif what == "o1":
                        dve.wait_ge(norm_act, at(turn, NORM_ACT, "o1"))
                        o0 = 2 * (h % 2)
                        v.tensor_tensor(zk[:, h, :], tmp[:, o0, :], tmp[:, o0 + 1, :], ALU.add).then_inc(norm_dve, 1)
                        dve.wait_ge(norm_act, at(turn, NORM_ACT, "q1"))
                        v.tensor_tensor(tmp[:, 4, :], tmp[:, 4, :], stat[:, :], ALU.add).then_inc(norm_dve, 1)
                    elif what == "stats":
                        dve.wait_ge(norm_act, at(turn, NORM_ACT, "msq"))
                        v.scalar_tensor_tensor(out=tmp[:, 4, :], in0=B_T[:, :], scalar=1.0 / HV, in1=stat[:, :],
                                               op0=ALU.mult, op1=ALU.subtract).then_inc(norm_dve, 1)
                        dve.wait_ge(norm_dve, at(turn, NORM_DVE, "var"))
                        v.tensor_scalar(tmp[:, 4, :], tmp[:, 4, :], 0.0, LN_EPS, ALU.max, ALU.add).then_inc(norm_dve, 1)
                        normalise(l, h)

            def pool_windows(l):
                done = l * WINDOW_STEPS
                dve.wait_ge(norm_dve, at(l * HEADS + HEADS - 1, NORM_DVE, "lo1"))
                for g, w in enumerate(WINDOWS):
                    u = u_p[:, g, :]
                    s = u
                    for i in range(g + 1):
                        step = 1 << i
                        to = win[:, i % 2, :]
                        v.tensor_tensor(to[:, step:S], s[:, step:S], s[:, 0:S - step], ALU.add).then_inc(win_dve, 1)
                        v.tensor_copy(to[:, 0:step], s[:, 0:step]).then_inc(win_dve, 1)
                        done += 2
                        dve.wait_ge(win_dve, done)
                        s = to
                    to = win[:, (g + 1) % 2, :]
                    v.tensor_scalar(to[:, w - 1:S], s[:, w - 1:S], 1.0 / w, None, ALU.mult).then_inc(win_dve, 1)
                    v.tensor_tensor(to[:, 0:w - 1], s[:, 0:w - 1], cinv[:, 0:w - 1], ALU.mult).then_inc(win_dve, 1)
                    dve.wait_ge(win_dve, done + 2)
                    v.tensor_tensor(u, to, u, ALU.subtract).then_inc(win_dve, 1)
                    done += 3
                    dve.wait_ge(win_dve, done)

            def mixer(l):
                v.memset(sc[:, :], 0.0).then_inc(sc_zero, 1)
                v.tensor_copy(layer_p[:, :], params[:, bass.ds(l * PER_LAYER + P_LAYER, PER_LAYER)])\
                    .then_inc(layer_copied, 1)
                dve.wait_ge(sc_zero, l + 1)
                dve.wait_ge(layer_copied, l + 1)
                nb = STAGE_BLOCKS
                for name, n, size, _ in MIX:
                    half = int(name[-1]) if name[-1].isdigit() else 0
                    group = GROUP0[1] + MIX_GROUP[name]
                    if name == "z":
                        for h in range(HEADS):
                            dve.wait_ge(z_pe, l * HEADS + h + 1 + HEADS)
                            v.tensor_scalar(zk[:, h, :], bank[h][:, :],
                                            layer_p[:, KT + POOL_GROUPS + h:KT + POOL_GROUPS + h + 1], None,
                                            ALU.add).then_inc(bank_read[h], 1)
                            dve.wait_ge(bank_read[h], read_in(l, group))
                    if name == "out0":
                        dve.wait_ge(quarter, quarters(l, STAGE_BLOCKS + MIX_FIRST["gp1"] + 1, TILE_N - 1))
                        clear_sums(l, 1)
                        coefficients(l, 1)
                    for b in range(n):
                        j = nb - STAGE_BLOCKS
                        if j > 0:
                            split_lo(l, nb + 1, MIX_SIZE[j + 1])
                        nb += 1
                        last = b == n - 1
                        if name[0] == "v":
                            prepare(l, 2 * half + b)
                        if name in GLA_GROUPS:
                            for f in range(TILE_N):
                                attend(l, GLA_GROUPS[name] + TILE_N * b + f)
                        if name == "gg0" and b == 0:
                            for f in range(TILE_N):
                                dve.wait_ge(bank_read[f], read_in(l, GROUP0[1] + MIX_GROUP["u"]))
                            pool_windows(l)
                        if name == "gg0" and last:
                            for g in range(POOL_GROUPS):
                                dve.wait_ge(p_hi_done, l * POOL_GROUPS + g + 1)
                                v.tensor_tensor(p_lo[:, g, :], u_p[:, g, :], p_hi[:, g, :].bitcast(F32),
                                                ALU.subtract).then_inc(p_ready, 1)
                        if name == "wp":
                            for f in range(TILE_N):
                                dve.wait_ge(quarter, quarters(l, nb - 1, f))
                                v.tensor_scalar(u_p[:, f, :], bank[f][:, :], layer_p[:, KT + f:KT + f + 1], None,
                                                ALU.mult).then_inc(bank_read[f], 1)
                            for f in range(TILE_N):
                                dve.wait_ge(pooled_hi_done, l * POOL_GROUPS + f + 1)
                                v.tensor_tensor(pooled_lo[:, f, :], u_p[:, f, :], pooled_hi[:, f, :].bitcast(F32),
                                                ALU.subtract).then_inc(pooled_ready, 1)
                        if name[:2] == "yg" and last:
                            for f in range(TILE_N):
                                dve.wait_ge(bank_read[f], free_for(l, group))
                                dve.wait_ge(quarter, quarters(l, nb - 1, f))
                                v.tensor_tensor(sg[:, f, :], sg[:, f, :], bank[f][:, :], ALU.mult)\
                                    .then_inc(bank_read[f], 1)
                        if name[:2] == "yp":
                            for f in range(TILE_N):
                                t = TILE_N * half + f
                                dve.wait_ge(bank_read[f], free_for(l, group))
                                dve.wait_ge(quarter, quarters(l, nb - 1, f))
                                v.tensor_tensor(sp_[:, f, :], sp_[:, f, :], bank[f][:, :], ALU.mult)\
                                    .then_inc(bank_read[f], 1)
                                dve.wait_ge(bank_read[f], read_in(l, group))
                                v.tensor_tensor(sp_[:, f, :], sp_[:, f, :], sg[:, f, :], ALU.add).then_inc(merged, 1)
                                if f:
                                    merge_low(l, t - 1)
                            merge_low(l, t)
                        if name[:3] == "out" and last:
                            residual(l, 1, group - half, nb - 1 - 2 * half, half, 2)
                layer_norm(l, 1)

            def merge_low(l, t):
                dve.wait_ge(m_hi_done, l * KT + t + 1)
                v.tensor_tensor(m_lo[:, t, :], sp_[:, t % TILE_N, :], m_hi[:, t, :].bitcast(F32),
                                ALU.subtract).then_inc(m_ready, 1)

            with dve.Fori(0, DEPTH) as l:
                ffn(l, 0)
                mixer(l)
                ffn(l, 2)

        @block.tensor
        def _(pe):
            mm = nc.tensor.matmul
            pe.sem_inc(quarter, 8)
            pe.sem_inc(ada_red, 2)
            pe.sem_inc(z_pe, HEADS)

            pe.wait_ge(consts, 7)
            pe.wait_ge(in_small, 16 * (2 + 3 * DEPTH + DEPTH + 1))
            nc.tensor.transpose(bank[4][:, 0:P], stage_rows[:, 0, :], ident[:, :]).then_inc(small_t, 1)
            n = N_MOD * KT + KT
            nc.tensor.transpose(bank[5][:, 0:n], stage_rows[0:n, 1, :], ident[0:n, 0:n]).then_inc(small_t, 1)
            n = N_MOD * KT
            nc.tensor.transpose(bank[6][:, 0:n], stage_rows[0:n, 2, :], ident[0:n, 0:n]).then_inc(small_t, 1)
            pe.wait_ge(in_x, 16 * PAIRS)
            for t in range(KT):
                if t >= TILE_N:
                    pe.wait_ge(x_r, t - TILE_N + 1)
                for a in range(PAIRS):
                    ins = nc.tensor.transpose(bank[t % TILE_N][:, a * P:(a + 1) * P],
                                              x_tok[:, a, t * P:(t + 1) * P], ident[:, :])
                ins.then_inc(x_t, 1)
            pe.wait_ge(c_ready, 1)
            for i in range(4):
                pe.wait_ge(in_ada[i], 16)
                for t in range(4):
                    for k in range(KT):
                        ins = mm(B_ADA[:, KT + 4 * i + t:KT + 4 * i + t + 1], ada_start[:, i, k, t * P:(t + 1) * P],
                                 c_act[:, k:k + 1], start=(k == 0), stop=(k == KT - 1))
            ins.then_inc(ada0, 1)

            def product(out_, w_, a_, start, stop, moving_w=False):
                (w1, w0), (a1, a0) = w_, a_
                if moving_w:
                    (w1, w0), (a1, a0) = (a1, a0), (w1, w0)
                mm(out_, w1, a1, start=start, stop=False)
                mm(out_, w1, a0, start=False, stop=False)
                return mm(out_, w0, a1, start=False, stop=stop)

            def weights(slot, k, f, width=512):
                c = slice(k * width + f * P, k * width + f * P + min(P, width))
                return wh[:, slot, c], wl[:, slot, c]

            def run_block(l, nb, a, ks, group, first, last, g=0, per=0, cols=(0, 1, 2, 3), k_outer=None, tokens=False,
                          behind=None):
                slot = nb % 2
                pe.wait_ge(w_lo, split_done(l, nb, g, per))

                def one(f, k):
                    start, stop = first and k == 0, last and k == ks - 1
                    if start:
                        pe.wait_ge(bank_read[f], free_for(l, group, g))
                    if tokens:
                        hi, lo = a(k)
                        at_f = slice(f * P, (f + 1) * P)
                        w = (wh[:, slot, k * 512:(k + 1) * 512], wl[:, slot, k * 512:(k + 1) * 512])
                        return product(bank[f][:, :], w, (hi[:, at_f], lo[:, at_f]), start, stop, moving_w=True)
                    return product(bank[f][:, :], weights(slot, k, cols[f]), a(k), start, stop)

                if k_outer:
                    for k in range(ks):
                        k_outer(k)
                        for f in range(TILE_N):
                            ins = one(f, k)
                            if k == ks - 1:
                                ins.then_inc(quarter, 1)
                    return
                for f in range(TILE_N):
                    for k in range(ks):
                        ins = one(f, k)
                    ins.then_inc(quarter, 1)
                    if behind:
                        behind(f)

            def h(b):
                return lambda k: (h_hi[:, 4 * b + k, :], h_lo[:, 4 * b + k, :])

            def h_there(l, s, b):
                return lambda k: pe.wait_ge(h_ready, (l * 3 + s) * KT + 4 * b + k + 1)

            def ada_pair(l, s, pair):
                if isinstance(pair, int) and pair == 0:
                    pe.wait_ge(coef, at(l * 3 + s, COEF, "mods"))
                for i in range(2):
                    pe.wait_ge(ada_step, l * (12 * ADA) + pair * 8 + 4 * (s * ADA + i) + 4)
                    mm(B_ADA[:, bass.ds(pair * 2 + i, 1)], ada[:, i, 0, :], ones[:, 0:1],
                       start=True, stop=True).then_inc(ada_red, 1)

            def norm_sums(l, s):
                pe.wait_ge(ln_sum, (l * 3 + s + 1) * (2 * KT) + 3)
                mm(B_OUT[:, :], ones[:, :], ln_acc[:, :], start=True, stop=True).then_inc(ln_pe, 1)
                pe.wait_ge(ln_sum, (l * 3 + s + 1) * (2 * KT) + 4)
                mm(B_KV[:, :], ones[:, :], ln_accq[:, :], start=True, stop=True).then_inc(ln_pe, 1)

            def ffn(l, s):
                base, group = STAGE_BLOCKS * s, GROUP0[s]
                up_cols = (0, 2, 1, 3)
                ada_pair(l, s, 0)
                for b in range(UP_BLOCKS):
                    run_block(l, base + b, h(b), 4, group, b == 0, b == 1, cols=up_cols, k_outer=h_there(l, s, b))
                ada_pair(l, s, 1)
                with pe.Fori(1, UP_GROUPS) as g:
                    for b in range(UP_BLOCKS):
                        run_block(l, base + b, h(b), 4, group, b == 0, b == 1, g, UP_BLOCKS, cols=up_cols)
                    ada_pair(l, s, g + 1)
                with pe.Fori(0, DOWN_GROUPS) as g:
                    k0 = 0
                    for b, ks in enumerate(DOWN_KS):
                        pe.wait_ge(act_ready, l * (2 * FT) + (s // 2) * FT + k0 + ks + 2)
                        run_block(l, base + DOWN0 + b, lambda k, k0=k0: (act_hi[:, k0 + k, :], act_lo[:, k0 + k, :]), ks,
                                  group + UP_GROUPS, b == 0, b == DOWN_BLOCKS - 1, g, DOWN_BLOCKS)
                        k0 += ks
                norm_sums(l, s)

            def attend(l, i):
                for what, hd in gla_slot(i):
                    turn = l * HEADS + hd
                    q, k, kend = qk[:, hd, 0, :], qk[:, hd, 1, :], zk[:, hd, :]
                    if what == "kT":
                        pe.wait_ge(prep_dve, at(turn, PREP_DVE, "kt"))
                        if hd >= 2:
                            pe.wait_ge(norm_dve, at(turn - 2, NORM_DVE, "var"))
                        for a in range(PAIRS):
                            ins = nc.tensor.transpose(B_T[:, a * P:(a + 1) * P], kend[:, a * P:(a + 1) * P], ident[:, :])
                        ins.then_inc(state_pe, 1)
                    elif what == "sc":
                        pe.wait_ge(kend_read, turn + 1)
                        for a in range(PAIRS):
                            at_a = slice(a * P, (a + 1) * P)
                            ins = mm(B_T[:, at_a], k[:, at_a], q[:, at_a], start=True, stop=True)
                        ins.then_inc(state_pe, 1)
                    elif what[:2] == "kv":
                        n = int(what[2])
                        if n:
                            pe.wait_ge(state_dve, at(turn, STATE_DVE, f"S{n - 1}" if n > 1 else "sc"))
                        rows = slice(n % 2 * CHUNK, (n % 2 + 1) * CHUNK)
                        mm((B_KV, B_T)[n % 2][:, 0:HV], kend_tok[rows, n // 2, :],
                           v_tok[rows, n // 2, hd * HV:(hd + 1) * HV], start=True, stop=True).then_inc(state_pe, 1)
                    elif what in ("o0", "o1"):
                        d = int(what[1])
                        pe.wait_ge(state_dve, at(turn, STATE_DVE, "S7"))
                        if d:
                            pe.wait_ge(norm_act, at(turn, NORM_ACT, "o0"))
                        elif hd:
                            pe.wait_ge(norm_act, at(turn - 1, NORM_ACT, "msq"))
                        cols = slice(hd * HV + d * P, hd * HV + (d + 1) * P)
                        for a in range(PAIRS):
                            at_a = slice(a * P, (a + 1) * P)
                            mm(B_OUT[:, at_a], v_tok[:, a, cols], sc[:, at_a], start=True, stop=False)
                            for n in (2 * a, 2 * a + 1):
                                if n:
                                    at_n = slice(n * CHUNK, (n + 1) * CHUNK)
                                    ins = mm(B_OUT[:, at_n], state[:, n, d * P:(d + 1) * P], q[:, at_n],
                                             start=False, stop=n == 2 * a + 1)
                        ins.then_inc(out_pe, 1)
                    elif what == "stats":
                        pe.wait_ge(norm_dve, at(turn, NORM_DVE, "osum"))
                        mm(B_OUT[:, :], ones[:, :], zk[:, hd, :], start=True, stop=True).then_inc(out_pe, 1)
                        if hd < HEADS - 1:
                            pe.wait_ge(state_dve, at(turn + 1, STATE_DVE, "S6"))
                        pe.wait_ge(norm_dve, at(turn, NORM_DVE, "sqsum"))
                        mm(B_T[:, :], ones[:, :], tmp[:, 4, :], start=True, stop=True).then_inc(out_pe, 1)

            def mixer(l):
                nb = STAGE_BLOCKS
                ada_pair(l, 1, 0)
                for name, n, size, pair in MIX:
                    group = GROUP0[1] + MIX_GROUP[name]
                    if name == "a":
                        pe.wait_ge(w_lo, split_done(l, nb))
                        for k in range(KT):
                            w = tuple(t[:, nb % 2, k * RANK:(k + 1) * RANK] for t in (wh, wl))
                            ins = product(B_T[0:RANK, :], w, (h_hi[:, k, :], h_lo[:, k, :]), k == 0, k == KT - 1)
                            if k % 2:
                                ins.then_inc(quarter, 1)
                        nb += 1
                        continue
                    if name == "z":
                        pe.wait_ge(a_act, l + 1)
                        pe.wait_ge(in_alpha, l * 16 + 16)
                        for hd in range(HEADS):
                            pe.wait_ge(bank_read[hd], free_for(l, group))
                            mm(bank[hd][:, :], alpha_w[:, hd * P:(hd + 1) * P], a_sb[:, :], start=True, stop=True)\
                                .then_inc(z_pe, 1)
                        continue
                    if name == "wp":
                        pe.wait_ge(w_lo, split_done(l, nb))
                        for g in range(POOL_GROUPS):
                            pe.wait_ge(bank_read[g], free_for(l, group))
                            pe.wait_ge(p_ready, l * POOL_GROUPS + g + 1)
                            product(bank[g][:, :], weights(nb % 2, g, 0, P), (p_hi[:, g, :], p_lo[:, g, :]),
                                    True, True).then_inc(quarter, 1)
                        nb += 1
                        continue
                    if name == "yg0":
                        pe.wait_ge(norm_dve, at(l * HEADS + HEADS - 1, NORM_DVE, "lo1"))
                    if name == "yp0":
                        pe.wait_ge(pooled_ready, l * POOL_GROUPS + POOL_GROUPS)
                    for b in range(n):
                        behind = k_outer = None
                        a = h(b)
                        if name == "q":
                            k_outer = h_there(l, 1, b)
                        elif name in GLA_GROUPS:
                            def behind(f, i=GLA_GROUPS[name] + TILE_N * b):
                                attend(l, i + f)
                        elif name[:2] == "yg":
                            def a(k, b=b):
                                return o_hi[:, 4 * b + k, :], o_lo[:, 4 * b + k, :]
                        elif name[:2] == "yp":
                            def a(k):
                                return pooled_hi[:, k, :], pooled_lo[:, k, :]
                        elif name[:3] == "out":
                            pe.wait_ge(m_ready, l * KT + 4 * b + 4)

                            def a(k, b=b):
                                return m_hi[:, 4 * b + k, :], m_lo[:, 4 * b + k, :]
                        run_block(l, nb, a, 4, group, b == 0, b == n - 1, k_outer=k_outer, tokens=name[0] == "v",
                                  behind=behind)
                        nb += 1
                    if pair:
                        ada_pair(l, 1, pair)
                norm_sums(l, 1)

            with pe.Fori(0, DEPTH) as l:
                ffn(l, 0)
                mixer(l)
                ffn(l, 2)
            for t in range(KT):
                pe.wait_ge(ln_act, at(3 * DEPTH - 1, LN_ACT, f"x{t}"))
                if t >= TILE_N:
                    pe.wait_ge(out_r, t - TILE_N + 1)
                for a in range(PAIRS):
                    ins = nc.tensor.transpose(bank[t % TILE_N][:, a * P:(a + 1) * P], xT[:, t, a * P:(a + 1) * P],
                                              ident[:, :])
                ins.then_inc(out_t, 1)


_INS = ["x", "c", "w_ada", "b_ada", "ffn1_up", "ffn1_down", "w_in", "w_alpha", "b_alpha", "gla_norm_g", "w_proj_gla",
        "w_pool", "pool_scale", "w_proj_pool", "w_out", "ffn2_up", "ffn2_down", "ln_g", "ln_b"]


def kernel(**inputs):
    import numpy as _np
    import concourse.bacc as _bacc
    from concourse import mybir as _mybir
    from concourse.bass_utils import run_bass_kernel_spmd as _run

    nc = _bacc.Bacc("TRN2", target_bir_lowering=False, num_devices=1)
    arrays, args = {}, []
    for name in _INS:
        a = _np.ascontiguousarray(inputs[name])
        arrays[f"in_{name}_dram"] = a
        args.append(nc.dram_tensor(f"in_{name}_dram", a.shape, _mybir.dt.from_np(a.dtype), kind="ExternalInput").ap())
    args.append(nc.dram_tensor("out_dram", (1, S, D), _mybir.dt.float32, kind="ExternalOutput").ap())
    trunk(nc, *args)
    r = _run(nc, [arrays], core_ids=[0])
    return r.results[0]["out_dram"]
```

```python
from contextlib import ExitStack

import concourse.bass as bass
from concourse import mybir

F32 = mybir.dt.float32
F32R = mybir.dt.float32r
I32 = mybir.dt.int32
ACT = mybir.ActivationFunctionType
ALU = mybir.AluOpType

P = 128
D = 1024
S = 512
DEPTH = 2
D_FF = 2816
DK = 512
HEADS = 4
DV = 1024
HV = DV // HEADS
RANK = 16
TAU = 16.0
CHUNK = 64
N_CHUNK = S // CHUNK
PAIRS = S // P
POOL_W = 512
POOL_GROUPS = 4
N_MOD = 9
ALPHA = (2 * DEPTH) ** 0.25
LN_EPS = 1e-5

KT = D // P
FT = D_FF // P
TILE_N = 4
SLOT = 4 * 512
HALF_SLOT = 2 * 512
NARROW = KT * RANK
SMALL = POOL_GROUPS * P

COL_Q, COL_K, COL_V, COL_R = 0, DK, 2 * DK, 2 * DK + DV
COL_A = COL_R + DV
COL_U = COL_A + RANK
COL_GG = COL_U + POOL_W
COL_GP = COL_GG + D

UP_GROUPS = FT // 2
UP_BLOCKS = 2
DOWN_KS = (4, 4, 2, 4, 4, 4)
DOWN_GROUPS = D // 512
DOWN_BLOCKS = len(DOWN_KS)
STAGE_BLOCKS = UP_GROUPS * UP_BLOCKS + DOWN_GROUPS * DOWN_BLOCKS
FFN_GROUPS = UP_GROUPS + DOWN_GROUPS
DOWN0 = UP_GROUPS * UP_BLOCKS
NB = 3 * STAGE_BLOCKS
MIX_GROUPS = 19
GROUP0 = (0, FFN_GROUPS, FFN_GROUPS + MIX_GROUPS)
NG = 2 * FFN_GROUPS + MIX_GROUPS

MIX = [
    ("q", 2, SLOT, 0), ("k", 2, SLOT, 1), ("a", 1, NARROW, None), ("z", 0, 0, None),
    ("v0", 2, SLOT, 2), ("v1", 2, SLOT, 3), ("r0", 2, SLOT, 4), ("r1", 2, SLOT, 5),
    ("u", 2, SLOT, 6), ("gg0", 2, SLOT, 7), ("wp", 1, SMALL, None), ("yg0", 2, SLOT, 8),
    ("gp0", 2, SLOT, 9), ("yp0", 1, SLOT, None), ("gg1", 2, SLOT, 10), ("yg1", 2, SLOT, 11),
    ("gp1", 2, SLOT, None), ("yp1", 1, SLOT, None), ("out0", 2, SLOT, None), ("out1", 2, SLOT, None),
]
MIX_FIRST = {}
MIX_GROUP = {}
_b = _g = 0
for _name, _n, _, _ in MIX:
    MIX_FIRST[_name], MIX_GROUP[_name] = _b, _g
    _b += _n
    _g += _name != "a"
assert _b == STAGE_BLOCKS and _g == MIX_GROUPS
MIX_SIZE = [size for _, n, size, _ in MIX for _ in range(n)] + [SLOT]

ADA = 3 * KT
ADA_PAIRS = ADA // 2

LOG_ACT = tuple(f"{w}{h}" for w in ("abs", "exp", "ln") for h in range(HEADS))
PREP_DVE = ("b", "to_end", "kend", "qt", "decay", "kt")
PREP_ACT = ("exp_b", "exp_nb", "exp_end")
STATE_PE = ("kT", "sc") + tuple(f"kv{c}" for c in range(N_CHUNK - 1))
STATE_DVE = ("sc",) + tuple(f"S{c}" for c in range(1, N_CHUNK))
OUT_PE = ("o0", "o1", "sum", "sq")
NORM_ACT = ("o0", "o1", "q0", "q1", "mean", "msq", "ln", "rstd")
NORM_DVE = ("osum", "sqsum", "var", "veps", "c0", "n0", "g0", "c1", "n1", "g1", "lo0", "lo1")
LN_PE = ("sum", "sq")
LN_ACT = ("mean", "msq", "ln", "rstd") + tuple(f"{w}{t}" for t in range(KT) for w in ("h", "hi", "x"))
LN_DVE = ("c0", "c1", "var", "veps", "n0") + tuple(
    f"{w}{t + (w == 'c')}" for t in range(1, KT) for w in "cn" if t + (w == "c") < KT)
ADA_DVE = (0, 2, 3)
COEF = ("mods", "gate", "scale1", "gs", "bs1", "bs", "lg", "lb")
WINDOWS = tuple(2 << g for g in range(POOL_GROUPS))
WINDOW_STEPS = sum(2 * (g + 1) + 3 for g in range(POOL_GROUPS))


def gla_slot(i):
    h, r = divmod(i, 4)
    steps = [[("o0", h - 1), ("kT", h)], [("o1", h - 1), ("sc", h), ("kv0", h)], [("kv1", h), ("kv2", h)],
             [("kv3", h), ("kv4", h), ("kv5", h), ("kv6", h), ("stats", h - 1)]][r]
    return [(w, n) for w, n in steps if 0 <= n < HEADS]


V_BLOCK_HEADS = ((None,), (0,), (1,), (2, 3))
GLA_GROUPS = {"r0": 0, "r1": 8, "u": 16}


def at(turn, steps, name):
    return turn * len(steps) + steps.index(name) + 1


def trunk(nc, x, c, w_ada, b_ada, ffn1_up, ffn1_down, w_in, w_alpha, b_alpha, gla_norm_g,
          w_proj_gla, w_pool, pool_scale, w_proj_pool, w_out, ffn2_up, ffn2_down, ln_g, ln_b, out):
    with ExitStack() as ctx:
        def sb(name, shape, dt=F32):
            return ctx.enter_context(nc.sbuf_tensor(name, shape, dt))

        def sem(name):
            return ctx.enter_context(nc.semaphore(name))

        def overlay(*specs):
            with ExitStack() as scope:
                return [scope.enter_context(nc.sbuf_tensor(n, s, dt)) for n, s, dt in specs]

        raw = sb("raw", [P, 2, SLOT])
        wh = sb("wh", [P, 2, SLOT], F32R)
        wl = sb("wl", [P, 2, SLOT], F32R)
        xT = sb("xT", [P, KT, S])
        ada = sb("ada", [P, 2, KT, P])
        alpha_w = sb("alpha_w", [RANK, DK])
        ones = sb("ones", [P, P])
        ident = sb("ident", [P, P])
        params = sb("params", [P, P])
        bias = sb("bias", [P, DEPTH * N_MOD * KT + 2 * KT])
        c_act = sb("c_act", [P, KT])
        cinv = sb("cinv", [P, WINDOWS[-1]])
        mods = sb("mods", [P, ADA])
        scale1 = sb("scale1", [P, KT])
        gate = sb("gate", [P, KT])
        gs = sb("gs", [P, KT])
        bs = sb("bs", [P, KT])
        lg = sb("lg", [P, KT])
        lb = sb("lb", [P, KT])
        layer_p = sb("layer_p", [P, KT + 2 * POOL_GROUPS])
        decay = sb("decay", [P, HEADS, N_CHUNK])
        touch = sb("touch", [P, 1])
        touch_v = sb("touch_v", [P, 1])
        mask = sb("mask", [P, P], mybir.dt.uint8)
        ln_acc, ln_accq, ln_sq = overlay(
            ("ln_acc", [P, S], F32), ("ln_accq", [P, S], F32), ("ln_sq", [P, 2, S], F32))
        h_hi = sb("h_hi", [P, KT, S], F32R)
        h_lo = sb("h_lo", [P, KT, S], F32R)
        x_tok, ada_start, stage_rows, maskf = overlay(
            ("x_tok", [P, PAIRS, D], F32), ("ada_start", [P, 4, KT, 512], F32),
            ("stage_rows", [P, 3, P], F32), ("maskf", [P, P], F32))
        _, out_tok = overlay(("gap4", [P, KT, S], F32), ("out_tok", [P, PAIRS, D], F32))
        mean, rstd, ln_tmp, ln_n, ln_h = overlay(
            ("mean", [P, S], F32), ("rstd", [P, S], F32), ("ln_tmp", [P, S], F32),
            ("ln_n", [P, 3, S], F32), ("ln_h", [P, 2, S], F32))
        act_hi, act_lo, silu = overlay(
            ("act_hi", [P, FT, S], F32R), ("act_lo", [P, FT, S], F32R), ("silu", [P, 2, S], F32))
        qk, _, v_tok, r_act, zk, state, kend_tok, sc, tmp, stat = overlay(
            ("qk", [P, HEADS, 2, S], F32), ("gap0", [P, KT, S], F32),
            ("v_tok", [P, PAIRS, DV], F32), ("r_act", [P, KT, S], F32), ("zk", [P, HEADS, S], F32),
            ("state", [P, N_CHUNK, HV], F32), ("kend_tok", [P, PAIRS, P], F32), ("sc", [P, S], F32),
            ("tmp", [P, 5, S], F32), ("stat", [P, S], F32))
        o_hi, o_lo = overlay(("o_hi", [P, KT, S], F32R), ("o_lo", [P, KT, S], F32R))
        _, u_p, p_hi, p_lo = overlay(
            ("gap1", [P, 2 * KT, S], F32), ("u_p", [P, POOL_GROUPS, S], F32),
            ("p_hi", [P, POOL_GROUPS, S], F32R), ("p_lo", [P, POOL_GROUPS, S], F32R))
        _, m_hi, m_lo, pooled_hi, pooled_lo, sg, sp_ = overlay(
            ("gap3", [P, 2 * KT, S], F32), ("m_hi", [P, KT, S], F32R), ("m_lo", [P, KT, S], F32R),
            ("pooled_hi", [P, POOL_GROUPS, S], F32R), ("pooled_lo", [P, POOL_GROUPS, S], F32R),
            ("sg", [P, TILE_N, S], F32), ("sp_", [P, TILE_N, S], F32))
        _, win, a_sb = overlay(("gap2", [P, 44, S], F32), ("win", [P, 2, S], F32), ("a_sb", [RANK, S], F32))
        sb("arena", [P, 48, S])

        bank = [ctx.enter_context(nc.psum_tensor(f"bank{i}", [P, S], F32)) for i in range(8)]
        B_OUT, B_KV, B_T, B_ADA = bank[4], bank[5], bank[6], bank[7]

        in_x = sem("in_x")
        in_mod = sem("in_mod")
        in_small = sem("in_small")
        in_ada = [sem(f"in_ada{i}") for i in range(4)]
        in_alpha = sem("in_alpha")
        landed = [[sem(f"landed{i}{j}") for j in range(2)] for i in range(2)]
        w_hi = sem("w_hi")
        w_lo = sem("w_lo")
        quarter = sem("quarter")
        bank_read = [sem(f"bank_read{i}") for i in range(TILE_N)]
        consts = sem("consts")
        c_ready = sem("c_ready")
        small_t = sem("small_t")
        small_r = sem("small_r")
        x_t = sem("x_t")
        x_r = sem("x_r")
        ada0_mul = sem("ada0_mul")
        ada0 = sem("ada0")
        first_mods = sem("first_mods")
        first_h, first_hi = sem("first_h"), sem("first_hi")
        h_ready = sem("h_ready")
        ada_in = [sem("ada_in0"), sem("ada_in1")]
        ada_step = sem("ada_step")
        ada_red = sem("ada_red")
        coef = sem("coef")
        act_hi_done = sem("act_hi_done")
        act_ready = sem("act_ready")
        ln_zero = sem("ln_zero")
        ln_sqd = sem("ln_sqd")
        ln_sum = sem("ln_sum")
        ln_pe, ln_act, ln_dve = sem("ln_pe"), sem("ln_act"), sem("ln_dve")
        a_act = sem("a_act")
        layer_copied = sem("layer_copied")
        z_pe = sem("z_pe")
        sc_zero = sem("sc_zero")
        log_act, log_a_done = sem("log_act"), sem("log_a_done")
        prep_dve, prep_act = sem("prep_dve"), sem("prep_act")
        state_pe, state_dve = sem("state_pe"), sem("state_dve")
        kend_read = sem("kend_read")
        out_pe, norm_act, norm_dve = sem("out_pe"), sem("norm_act"), sem("norm_dve")
        o_hi_done = sem("o_hi_done")
        win_dve = sem("win_dve")
        p_hi_done, p_ready = sem("p_hi_done"), sem("p_ready")
        pooled_hi_done, pooled_ready = sem("pooled_hi_done"), sem("pooled_ready")
        merged, m_hi_done, m_ready = sem("merged"), sem("m_hi_done"), sem("m_ready")
        out_t, out_r, stored = sem("out_t"), sem("out_r"), sem("stored")

        def block_no(l, nb, g=0, per=0):
            return l * NB + g * per + nb

        def split_done(l, nb, g=0, per=0):
            return block_no(l, nb, g, per) + 3

        def quarters(l, nb, f, g=0, per=0):
            return l * (4 * NB) + g * (4 * per) + 4 * nb + f + 1 + 8

        def landings(l, nb, g=0, per=0):
            return l * (8 * NB) + g * (8 * per) + 16 * (nb // 2 + 1)

        def free_for(l, group, g=0):
            return l * NG + g + group + 1

        def read_in(l, group, g=0):
            return free_for(l, group, g) + 1

        def tile(t, i):
            if isinstance(i, int):
                return t[:, i, :]
            return t[:, bass.ds(i, 1), :].rearrange("p a s -> p (a s)")

        P_LAYER = 2 * DEPTH * 3 * KT
        PER_LAYER = KT + 2 * POOL_GROUPS

        up = [ffn1_up.rearrange("l (k p) (h n) -> l p k h n", p=P, h=2), None,
              ffn2_up.rearrange("l (k p) (h n) -> l p k h n", p=P, h=2)]
        down = [ffn1_down.rearrange("l (k p) n -> l p k n", p=P), None,
                ffn2_down.rearrange("l (k p) n -> l p k n", p=P)]
        win_v = w_in.rearrange("l (k p) n -> l p k n", p=P)
        pg_v = w_proj_gla.rearrange("l (k p) n -> l p k n", p=P)
        pp_v = w_proj_pool.rearrange("l (k p) n -> l p k n", p=P)
        wo_v = w_out.rearrange("l (k p) n -> l p k n", p=P)
        wpool_v = w_pool.rearrange("l g i o -> l i g o")
        ada_v = w_ada.rearrange("l (k p) n -> l p k n", p=P)

        block = ctx.enter_context(nc.Block())

        @block.sync
        def _(sp):
            rows = N_MOD * KT
            sp.dma_start(stage_rows[rows:rows + KT, 1, :], c.rearrange("a (t p) -> (a t) p", p=P)).then_inc(in_mod, 16)
            sp.dma_start(stage_rows[0:rows, 1, :], b_ada[0].rearrange("(t p) -> t p", p=P)).then_inc(in_mod, 16)
            for t in range(PAIRS):
                sp.dma_start(x_tok[:, t, :], x[0, t * P:(t + 1) * P, :]).then_inc(in_x, 16)
            for i in range(4):
                sp.dma_start(ada_start[:, i, :, :], ada_v[0, :, :, i * 512:(i + 1) * 512])\
                    .then_inc(in_ada[i], 16)

            def load(src, l, nb, size, g=0, per=0, width=512):
                sp.wait_ge(w_lo, block_no(l, nb, g, per) + 1)
                slot = nb % 2
                for i in range(2):
                    if width == "gate/up":
                        dst = raw[:, slot, 0:size].rearrange("p (k h n) -> p k h n", h=2, n=2 * P)[:, :, i, :]
                        part = src[:, :, i, :]
                    else:
                        dst = raw[:, slot, i * size // 2:(i + 1) * size // 2].rearrange("p (k n) -> p k n", n=width)
                        ks = size // width
                        part = src[:, i * ks // 2:(i + 1) * ks // 2, :]
                    sp.dma_start(dst, part).then_inc(landed[slot][i], 16)

            def load_ffn(l, s):
                base = STAGE_BLOCKS * s
                with sp.Fori(0, UP_GROUPS) as g:
                    for b in range(UP_BLOCKS):
                        load(up[s][l, :, 4 * b:4 * b + 4, :, bass.ds(g * (2 * P), 2 * P)], l, base + b, SLOT,
                             g, UP_BLOCKS, width="gate/up")
                with sp.Fori(0, DOWN_GROUPS) as g:
                    k0 = 0
                    for b, ks in enumerate(DOWN_KS):
                        load(down[s][l, :, k0:k0 + ks, bass.ds(g * 512, 512)], l, base + DOWN0 + b,
                             ks * 512, g, DOWN_BLOCKS)
                        k0 += ks

            def load_mix(l):
                sp.wait_ge(z_pe, l * HEADS + HEADS)
                sp.dma_start(alpha_w[:, :], w_alpha[l]).then_inc(in_alpha, 16)
                nb = STAGE_BLOCKS
                for name, n, size, _ in MIX:
                    for b in range(n):
                        ks = slice(4 * b, 4 * b + 4)
                        half = int(name[-1]) * 512 if name[-1].isdigit() else 0
                        if name == "a":
                            src, w = win_v[l, :, :, COL_A:COL_A + RANK], RANK
                        elif name == "wp":
                            src, w = wpool_v[l], P
                        elif name[:2] == "yg":
                            src, w = pg_v[l, :, ks, half:half + 512], 512
                        elif name[:2] == "yp":
                            src, w = pp_v[l, :, :, half:half + 512], 512
                        elif name[:3] == "out":
                            src, w = wo_v[l, :, ks, half:half + 512], 512
                        else:
                            col = {"q": COL_Q, "k": COL_K, "v": COL_V, "r": COL_R, "u": COL_U,
                                   "gg": COL_GG, "gp": COL_GP}[name.rstrip("01")] + half
                            src, w = win_v[l, :, ks, col:col + 512], 512
                        load(src, l, nb, size, width=w)
                        nb += 1

            with sp.Fori(0, DEPTH) as l:
                load_ffn(l, 0)
                load_mix(l)
                load_ffn(l, 2)
            for b in range(2):
                load(wo_v[0, :, 0:4, 0:512], DEPTH, b, SLOT)
            for part in range(4):
                sp.wait_ge(out_r, 2 * part + 2)
                cols = slice(part * 2 * P, (part + 1) * 2 * P)
                sp.dma_start(out[0].rearrange("(a p) n -> p a n", p=P)[:, :, cols], out_tok[:, :, cols])\
                    .then_inc(stored, 16)
            sp.wait_ge(stored, 16 * 4)

        @block.gpsimd
        def _(pool):
            nc.gpsimd.memset(ones[:, :], 1.0).then_inc(consts, 1)
            nc.gpsimd.memset(ident[:, :], 0.0).then_inc(consts, 1)
            pool.wait_ge(consts, 2)
            nc.gpsimd.affine_select(out=ident[:, :], in_=ident[:, :], compare_op=ALU.not_equal, fill=1.0,
                                    base=0, pattern=[[-1, P]], channel_multiplier=1).then_inc(consts, 1)
            nc.gpsimd.affine_select(out=maskf[:, :], in_=ones[:, :], compare_op=ALU.is_ge, fill=0.0,
                                    base=0, pattern=[[1, P]], channel_multiplier=-1).then_inc(consts, 1)
            pool.wait_ge(consts, 4)
            nc.gpsimd.memset(maskf[0:CHUNK, CHUNK:P], 0.0).then_inc(consts, 1)
            pool.wait_ge(consts, 5)
            nc.gpsimd.tensor_copy(mask[:, :], maskf[:, :]).then_inc(consts, 1)
            for i in range(WINDOWS[-1]):
                last = nc.gpsimd.memset(cinv[:, i:i + 1], 1.0 / (i + 1))
            last.then_inc(consts, 1)
            row = 0
            srcs = [ln_g.rearrange("l s (t p) -> (l s t) p", p=P), ln_b.rearrange("l s (t p) -> (l s t) p", p=P)]
            for l in range(DEPTH):
                srcs += [gla_norm_g[l].rearrange("h (t p) -> (h t) p", p=P),
                         pool_scale[l].rearrange("(t p) -> t p", p=P), b_alpha[l].rearrange("(t p) -> t p", p=P)]
            for src in srcs:
                n = src.shape[0]
                pool.dma_start(stage_rows[row:row + n, 0, :], src).then_inc(in_small, 16)
                row += n
            pool.dma_start(stage_rows[0:N_MOD * KT, 2, :],
                           b_ada[1].rearrange("(t p) -> t p", p=P)).then_inc(in_small, 16)

            pool.wait_ge(c_ready, 1)

            def columns(src_l, col0, g, first, per_layer, l):
                for i in range(2):
                    pool.wait_ge(ada_red, l * per_layer + g * 2 + (first + i) + 1)
                    pool.dma_start(ada[:, i, :, :], ada_v[src_l, :, :, bass.ds(g * (2 * P) + (col0 + i * P), P)])\
                        .then_inc(ada_in[i], 16)
                for i in range(2):
                    done = l * (4 * per_layer) + g * 8 + 4 * (first + i)
                    pool.wait_ge(ada_in[i], l * (8 * per_layer) + g * 16 + 8 * first + 16)
                    nc.gpsimd.tensor_tensor(ada[:, i, :, :], ada[:, i, :, :],
                                            c_act[:, :].unsqueeze(2).to_broadcast([P, KT, P]), ALU.mult)\
                        .then_inc(ada_step, 1)
                    for n, w in enumerate((KT // 2, KT // 4, KT // 8)):
                        pool.wait_ge(ada_step, done + n + 1)
                        nc.gpsimd.tensor_tensor(ada[:, i, 0:w, :], ada[:, i, 0:w, :], ada[:, i, w:2 * w, :],
                                                ALU.add).then_inc(ada_step, 1)

            here = (N_MOD - 2) * KT
            with pool.Fori(0, DEPTH) as l:
                with pool.Fori(0, here // 2) as g:
                    columns(l, 2 * D, g, 0, 3 * ADA, l)
                with pool.Fori(0, KT) as g:
                    columns((l + 1) % DEPTH, 0, g, here, 3 * ADA, l)

        @block.scalar
        def _(act):
            for f in range(TILE_N):
                act.sem_inc(bank_read[f], 1)
            copy = nc.scalar.copy

            def split_hi(l, nb, size, g=0, per=0):
                slot = nb % 2
                for half in range(2):
                    act.wait_ge(landed[slot][half], landings(l, nb, g, per))
                act.wait_ge(quarter, quarters(l, nb - 2, TILE_N - 1, g, per))
                copy(wh[:, slot, 0:size], raw[:, slot, 0:size]).then_inc(w_hi, 1)

            def touch_table(func):
                nc.scalar.activation(touch[:, :], ones[:, 0:1], func)

            n = N_MOD * KT
            act.wait_ge(small_t, 1)
            nc.scalar.activation(c_act[:, :], bank[5][:, n:n + KT], ACT.Silu).then_inc(c_ready, 1)
            copy(bias[:, 0:n], bank[5][:, 0:n]).then_inc(small_r, 1)
            for t in range(KT):
                act.wait_ge(x_t, t + 1)
                copy(xT[:, t, :], bank[t % TILE_N][:, :]).then_inc(x_r, 1)
            split_hi(0, 0, SLOT)
            split_hi(0, 1, SLOT)
            act.wait_ge(small_t, 3)
            copy(params[:, :], bank[4][:, 0:P]).then_inc(small_r, 1)
            copy(bias[:, n:2 * n], bank[6][:, 0:n]).then_inc(small_r, 1)
            for t in range(KT):
                act.wait_ge(first_h, t + 1)
                copy(h_hi[:, t, :], ln_h[:, t % 2, :]).then_inc(first_hi, 1)

            def squares(l, s, group, g=0):
                for f in range(TILE_N):
                    act.wait_ge(bank_read[f], read_in(l, group, g))
                    act.wait_ge(ln_sum, l * (6 * KT) + g * (2 * TILE_N) + 2 * (s * KT + f) + 2)
                    nc.scalar.activation(ln_sq[:, f % 2, :], tile(xT, g * TILE_N + f), ACT.Square)\
                        .then_inc(ln_sqd, 1)

            def layer_norm(l, s):
                turn = l * 3 + s
                act.wait_ge(ln_pe, at(turn, LN_PE, "sum"))
                nc.scalar.activation(mean[:, :], B_OUT[:, :], ACT.Copy, scale=1.0 / D).then_inc(ln_act, 1)
                nc.scalar.activation(ln_tmp[:, :], B_OUT[:, :], ACT.Square, scale=1.0 / D).then_inc(ln_act, 1)
                act.wait_ge(ln_dve, at(turn, LN_DVE, "veps"))
                nc.scalar.activation(rstd[:, :], rstd[:, :], ACT.Ln).then_inc(ln_act, 1)
                act.wait_ge(ln_act, at(turn, LN_ACT, "ln"))
                nc.scalar.activation(rstd[:, :], rstd[:, :], ACT.Exp, scale=-0.5).then_inc(ln_act, 1)
                for t in range(KT):
                    act.wait_ge(ln_dve, at(turn, LN_DVE, f"n{t}"))
                    if t >= 2:
                        act.wait_ge(h_ready, l * (3 * KT) + (s + 1) * KT + t - 1)
                    nc.scalar.activation(ln_h[:, t % 2, :], ln_n[:, t % 3, :], ACT.Identity,
                                         bias=bs[:, t:t + 1], scale=gs[:, t:t + 1]).then_inc(ln_act, 1)
                    act.wait_ge(ln_act, at(turn, LN_ACT, f"h{t}"))
                    copy(h_hi[:, t, :], ln_h[:, t % 2, :]).then_inc(ln_act, 1)
                    nc.scalar.activation(xT[:, t, :], ln_n[:, t % 3, :], ACT.Identity,
                                         bias=lb[:, t:t + 1], scale=lg[:, t:t + 1]).then_inc(ln_act, 1)
                    if t == 1:
                        split_hi(l, STAGE_BLOCKS * (s + 1) + 1, SLOT)
                act.wait_ge(ln_act, at(turn, LN_ACT, f"x{KT - 1}"))
                touch_table(ACT.Silu)

            def hidden(l, s, g):
                group, last = GROUP0[s], STAGE_BLOCKS * s + 1
                for i in range(2):
                    f = 2 * i
                    n = l * (2 * FT) + (s // 2) * FT + 2 * g + i
                    act.wait_ge(quarter, quarters(l, last, f, g, UP_BLOCKS))
                    act.wait_ge(act_ready, n + 1)
                    nc.scalar.activation(silu[:, i, :], bank[f][:, :], ACT.Silu).then_inc(bank_read[f], 1)
                    act.wait_ge(bank_read[f + 1], read_in(l, group, g))
                    copy(tile(act_hi, 2 * g + i), silu[:, i, :]).then_inc(act_hi_done, 1)

            def ffn(l, s):
                base = STAGE_BLOCKS * s
                split_hi(l, base + 2, SLOT)
                hidden(l, s, 0)
                with act.Fori(1, UP_GROUPS) as g:
                    split_hi(l, base + 1, SLOT, g, UP_BLOCKS)
                    split_hi(l, base + 2, SLOT, g, UP_BLOCKS)
                    hidden(l, s, g)
                touch_table(ACT.Ln)
                with act.Fori(0, DOWN_GROUPS) as g:
                    for b in range(DOWN_BLOCKS):
                        size = DOWN_KS[(b + 1) % DOWN_BLOCKS] * 512
                        split_hi(l, base + DOWN0 + b + 1, size, g, DOWN_BLOCKS)
                    squares(l, s, GROUP0[s] + UP_GROUPS, g)
                layer_norm(l, s)

            def log_decays(l):
                for h in range(HEADS):
                    act.wait_ge(bank_read[h], read_in(l, GROUP0[1] + MIX_GROUP["z"]))
                    nc.scalar.activation(tmp[:, h, :], zk[:, h, :], ACT.Abs).then_inc(log_act, 1)
                for h in range(HEADS):
                    act.wait_ge(log_act, at(l, LOG_ACT, f"abs{h}"))
                    nc.scalar.activation(tmp[:, h, :], tmp[:, h, :], ACT.Exp, scale=-1.0).then_inc(log_act, 1)
                for h in range(HEADS):
                    act.wait_ge(log_act, at(l, LOG_ACT, f"exp{h}"))
                    nc.scalar.activation(tmp[:, h, :], tmp[:, h, :], ACT.Ln, bias=1.0).then_inc(log_act, 1)
                touch_table(ACT.Exp)

            def prepare(l, h):
                turn = l * HEADS + h
                act.wait_ge(prep_dve, at(turn, PREP_DVE, "b"))
                nc.scalar.activation(tmp[:, 0, :], tmp[:, 3, :], ACT.Exp, scale=1.0 / TAU).then_inc(prep_act, 1)
                nc.scalar.activation(tmp[:, 1, :], tmp[:, 3, :], ACT.Exp, scale=-1.0 / TAU).then_inc(prep_act, 1)
                act.wait_ge(prep_dve, at(turn, PREP_DVE, "to_end"))
                nc.scalar.activation(tmp[:, 2, :], tmp[:, 2, :], ACT.Exp, scale=1.0 / TAU).then_inc(prep_act, 1)

            def high_of_output(l, h):
                turn = l * HEADS + h
                for d in range(2):
                    act.wait_ge(norm_dve, at(turn, NORM_DVE, f"g{d}"))
                    copy(o_hi[:, 2 * h + d, :], tmp[:, 2 * (h % 2) + d, :]).then_inc(o_hi_done, 1)

            def deviation(l, h):
                turn = l * HEADS + h
                act.wait_ge(norm_dve, at(turn, NORM_DVE, "veps"))
                nc.scalar.activation(tmp[:, 4, :], tmp[:, 4, :], ACT.Ln).then_inc(norm_act, 1)
                act.wait_ge(norm_act, at(turn, NORM_ACT, "ln"))
                nc.scalar.activation(tmp[:, 4, :], tmp[:, 4, :], ACT.Exp, scale=-0.5).then_inc(norm_act, 1)

            def attend(l, i):
                for what, h in gla_slot(i):
                    turn = l * HEADS + h
                    out0 = 2 * (h % 2)
                    if what == "kT":
                        act.wait_ge(state_pe, at(turn, STATE_PE, "kT"))
                        copy(kend_tok[:, :, :], B_T[:, :].rearrange("p (a d) -> p a d", d=P)).then_inc(kend_read, 1)
                    elif what == "o0":
                        act.wait_ge(out_pe, at(turn, OUT_PE, "o0"))
                        if h >= 2:
                            act.wait_ge(norm_dve, at(turn - 2, NORM_DVE, "lo1"))
                        copy(tmp[:, out0, :], B_OUT[:, :]).then_inc(norm_act, 1)
                    elif what == "o1":
                        act.wait_ge(out_pe, at(turn, OUT_PE, "o1"))
                        copy(tmp[:, out0 + 1, :], B_OUT[:, :]).then_inc(norm_act, 1)
                        if h:
                            act.wait_ge(norm_dve, at(turn - 1, NORM_DVE, "n1"))
                        act.wait_ge(norm_act, at(turn, NORM_ACT, "o1"))
                        nc.scalar.activation(tmp[:, 4, :], tmp[:, out0, :], ACT.Square).then_inc(norm_act, 1)
                        nc.scalar.activation(stat[:, :], tmp[:, out0 + 1, :], ACT.Square).then_inc(norm_act, 1)
                    elif what == "stats":
                        act.wait_ge(out_pe, at(turn, OUT_PE, "sq"))
                        nc.scalar.activation(zk[:, h, :], B_OUT[:, :], ACT.Copy, scale=1.0 / HV).then_inc(norm_act, 1)
                        nc.scalar.activation(stat[:, :], B_OUT[:, :], ACT.Square, scale=1.0 / HV).then_inc(norm_act, 1)

            def mixer(l):
                nb = STAGE_BLOCKS
                for name, n, size, _ in MIX:
                    half = int(name[-1]) if name[-1].isdigit() else 0
                    group = GROUP0[1] + MIX_GROUP[name]
                    for b in range(n):
                        j = nb - STAGE_BLOCKS
                        if j > 0:
                            split_hi(l, nb + 1, MIX_SIZE[j + 1])
                        nb += 1
                        last = b == n - 1
                        if name == "out0" and b == 0:
                            touch_table(ACT.Ln)
                        for h in V_BLOCK_HEADS[2 * half + b] if name[0] == "v" else ():
                            if h is None:
                                log_decays(l)
                            elif h < HEADS - 1:
                                prepare(l, h)
                        summed = (GLA_GROUPS[name] + TILE_N * b) // 4 - 2 if name in GLA_GROUPS else -1
                        if summed >= 0:
                            deviation(l, summed)
                        if name == "gg0" and last:
                            act.wait_ge(norm_dve, at(l * HEADS + HEADS - 1, NORM_DVE, "lo1"))
                        if name in ("gg1", "gp1") and last:
                            act.wait_ge(merged, l * KT + TILE_N)
                        for f in range(TILE_N):
                            if name == "gg0" and last:
                                act.wait_ge(win_dve, l * WINDOW_STEPS + sum(2 * (i + 1) + 3 for i in range(f + 1)))
                                copy(p_hi[:, f, :], u_p[:, f, :]).then_inc(p_hi_done, 1)
                            if name == "v1" and last and f == TILE_N - 1:
                                prepare(l, HEADS - 1)
                            if last and name not in ("a", "wp", "yg0", "yg1", "yp0", "yp1", "out0", "out1"):
                                act.wait_ge(quarter, quarters(l, nb - 1, f))
                                kind = name.rstrip("01")
                                if kind == "q":
                                    ins = copy(qk[:, f, 0, :], bank[f][:, :])
                                elif kind == "k":
                                    ins = copy(qk[:, f, 1, :], bank[f][:, :])
                                elif kind == "v":
                                    ins = copy(v_tok[:, f, half * 512:half * 512 + 512], bank[f][:, :])
                                elif kind == "r":
                                    ins = nc.scalar.activation(r_act[:, TILE_N * half + f, :], bank[f][:, :], ACT.Silu)
                                elif kind == "u":
                                    ins = copy(u_p[:, f, :], bank[f][:, :])
                                else:
                                    dst = sg if kind == "gg" else sp_
                                    ins = nc.scalar.activation(dst[:, f, :], bank[f][:, :], ACT.Sigmoid)
                                ins.then_inc(bank_read[f], 1)
                            if name in GLA_GROUPS:
                                attend(l, GLA_GROUPS[name] + TILE_N * b + f)
                            if f == 0 and summed >= 0:
                                high_of_output(l, summed)
                        if name == "a":
                            act.wait_ge(quarter, quarters(l, nb - 1, TILE_N - 1))
                            copy(a_sb[:, :], B_T[0:RANK, :]).then_inc(a_act, 1)
                        if name == "wp":
                            for f in range(TILE_N):
                                act.wait_ge(bank_read[f], read_in(l, group))
                                copy(pooled_hi[:, f, :], u_p[:, f, :]).then_inc(pooled_hi_done, 1)
                        if name[:2] == "yp":
                            for f in range(TILE_N):
                                act.wait_ge(merged, l * KT + TILE_N * half + f + 1)
                                copy(m_hi[:, TILE_N * half + f, :], sp_[:, f, :]).then_inc(m_hi_done, 1)
                        if name[:3] == "out" and last:
                            squares(l, 1, GROUP0[1] + MIX_GROUP["out0"], half)
                layer_norm(l, 1)

            with act.Fori(0, DEPTH) as l:
                ffn(l, 0)
                mixer(l)
                ffn(l, 2)
            for t in range(KT):
                act.wait_ge(out_t, t + 1)
                copy(out_tok[:, :, t * P:(t + 1) * P], bank[t % TILE_N][:, :].rearrange("p (a d) -> p a d", d=P))\
                    .then_inc(out_r, 1)

        @block.vector
        def _(dve):
            v = nc.vector
            dve.sem_inc(w_lo, 2)
            dve.sem_inc(act_ready, 2)
            dve.sem_inc(ln_sum, 4)

            def split_lo(l, nb, size, g=0, per=0):
                slot = nb % 2
                dve.wait_ge(w_hi, block_no(l, nb, g, per) + 1)
                v.tensor_tensor(wl[:, slot, 0:size], raw[:, slot, 0:size], wh[:, slot, 0:size].bitcast(F32),
                                ALU.subtract).then_inc(w_lo, 1)

            v.memset(bias[:, 2 * N_MOD * KT:], 0.0)
            dve.wait_ge(c_ready, 1)
            for n, i in enumerate(ADA_DVE):
                dve.wait_ge(in_ada[i], 16)
                total = ada_start[:, i, 0, :]
                v.tensor_scalar(total, total, c_act[:, 0:1], None, ALU.mult).then_inc(ada0_mul, 1)
                for k in range(1, KT):
                    dve.wait_ge(ada0_mul, n * KT + k)
                    v.scalar_tensor_tensor(out=total, in0=ada_start[:, i, k, :], scalar=c_act[:, k:k + 1],
                                           in1=total, op0=ALU.mult, op1=ALU.add).then_inc(ada0_mul, 1)
            split_lo(0, 0, SLOT)
            dve.wait_ge(small_r, 1)
            dve.wait_ge(ada0, 4)
            v.tensor_tensor(mods[:, KT:ADA], B_ADA[:, KT:ADA], bias[:, 0:2 * KT], ALU.add).then_inc(first_mods, 1)
            dve.wait_ge(first_mods, 1)
            v.tensor_scalar(scale1[:, :], mods[:, 2 * KT:ADA], 1.0, None, ALU.add).then_inc(first_mods, 1)
            dve.wait_ge(first_mods, 2)
            dve.sem_inc(coef, len(COEF))
            dve.wait_ge(x_r, KT)
            for t in range(KT):
                if t >= 2:
                    dve.wait_ge(h_ready, t - 1)
                v.tensor_scalar(ln_h[:, t % 2, :], xT[:, t, :], scale1[:, t:t + 1], mods[:, KT + t:KT + t + 1],
                                ALU.mult, ALU.add).then_inc(first_h, 1)
                dve.wait_ge(first_hi, t + 1)
                v.tensor_tensor(h_lo[:, t, :], ln_h[:, t % 2, :], h_hi[:, t, :].bitcast(F32),
                                ALU.subtract).then_inc(h_ready, 1)
                if t == 3:
                    split_lo(0, 1, SLOT)
            dve.wait_ge(small_r, 3)
            dve.wait_ge(consts, 7)

            def coefficients(l, s):
                turn = l * 3 + s
                half = 1.0 if s == 1 else 0.5
                dve.wait_ge(ada_red, (turn + 1) * ADA + 2)

                def done(name):
                    return at(turn + 1, COEF, name)
                v.tensor_tensor(mods[:, :], B_ADA[:, 0:ADA],
                                bias[:, bass.ds(l * (N_MOD * KT) + (3 * s + 2) * KT, ADA)], ALU.add).then_inc(coef, 1)
                dve.wait_ge(coef, done("mods"))
                v.tensor_scalar(gate[:, :], mods[:, 0:KT], 1.0, half / ALPHA, ALU.add, ALU.mult).then_inc(coef, 1)
                v.tensor_scalar(scale1[:, :], mods[:, 2 * KT:ADA], 1.0, None, ALU.add).then_inc(coef, 1)
                dve.wait_ge(coef, done("scale1"))
                ln_gain = params[:, bass.ds(l * (3 * KT) + s * KT, KT)]
                ln_bias = params[:, bass.ds(l * (3 * KT) + (DEPTH * 3 + s) * KT, KT)]
                v.tensor_tensor(gs[:, :], scale1[:, :], ln_gain, ALU.mult).then_inc(coef, 1)
                v.tensor_tensor(bs[:, :], scale1[:, :], ln_bias, ALU.mult).then_inc(coef, 1)
                dve.wait_ge(coef, done("bs1"))
                v.tensor_tensor(bs[:, :], bs[:, :], mods[:, KT:2 * KT], ALU.add).then_inc(coef, 1)
                v.tensor_copy(lg[:, :], ln_gain).then_inc(coef, 1)
                v.tensor_copy(lb[:, :], ln_bias).then_inc(coef, 1)

            def clear_sums(l, s):
                v.memset(ln_acc[:, :], 0.0).then_inc(ln_zero, 1)
                v.memset(ln_accq[:, :], 0.0).then_inc(ln_zero, 1)
                dve.wait_ge(ln_zero, (l * 3 + s) * 2 + 2)

            def residual(l, s, group, last, g=0, per=0):
                for f in range(TILE_N):
                    n = l * (6 * KT) + g * (2 * TILE_N) + 2 * (s * KT + f) + 4
                    t = g * TILE_N + f
                    dve.wait_ge(quarter, quarters(l, last, f, g, per))
                    v.scalar_tensor_tensor(out=tile(xT, t), in0=bank[f][:, :],
                                           scalar=gate[:, bass.ds(t, 1)], in1=tile(xT, t),
                                           op0=ALU.mult, op1=ALU.add).then_inc(bank_read[f], 1)
                    dve.wait_ge(bank_read[f], read_in(l, group, g))
                    dve.wait_ge(ln_sum, n)
                    v.tensor_tensor(ln_acc[:, :], ln_acc[:, :], tile(xT, t), ALU.add).then_inc(ln_sum, 1)
                    dve.wait_ge(ln_sqd, l * (3 * KT) + g * TILE_N + s * KT + f + 1)
                    v.tensor_tensor(ln_accq[:, :], ln_accq[:, :], ln_sq[:, f % 2, :], ALU.add).then_inc(ln_sum, 1)

            def layer_norm(l, s):
                turn = l * 3 + s

                def low(t):
                    dve.wait_ge(ln_act, at(turn, LN_ACT, f"hi{t}"))
                    v.tensor_tensor(h_lo[:, t, :], ln_h[:, t % 2, :], h_hi[:, t, :].bitcast(F32),
                                    ALU.subtract).then_inc(h_ready, 1)

                def centre(t):
                    if t >= 3:
                        dve.wait_ge(ln_act, at(turn, LN_ACT, f"x{t - 3}"))
                    v.tensor_tensor(ln_n[:, t % 3, :], xT[:, t, :], mean[:, :], ALU.subtract).then_inc(ln_dve, 1)

                def scaled(t):
                    if t == 0:
                        dve.wait_ge(ln_act, at(turn, LN_ACT, "rstd"))
                    dve.wait_ge(ln_dve, at(turn, LN_DVE, f"c{t}"))
                    v.tensor_tensor(ln_n[:, t % 3, :], ln_n[:, t % 3, :], rstd[:, :], ALU.mult).then_inc(ln_dve, 1)

                dve.wait_ge(coef, at(turn + 1, COEF, "lb"))
                dve.wait_ge(ln_act, at(turn, LN_ACT, "mean"))
                centre(0)
                centre(1)
                dve.wait_ge(ln_pe, at(turn, LN_PE, "sq"))
                dve.wait_ge(ln_act, at(turn, LN_ACT, "msq"))
                v.scalar_tensor_tensor(out=rstd[:, :], in0=B_KV[:, :], scalar=1.0 / D, in1=ln_tmp[:, :],
                                       op0=ALU.mult, op1=ALU.subtract).then_inc(ln_dve, 1)
                dve.wait_ge(ln_dve, at(turn, LN_DVE, "var"))
                v.tensor_scalar(rstd[:, :], rstd[:, :], 0.0, LN_EPS / ALPHA ** 2, ALU.max, ALU.add).then_inc(ln_dve, 1)
                scaled(0)
                for t in range(1, KT):
                    if t < KT - 1:
                        centre(t + 1)
                    scaled(t)
                    low(t - 1)
                    if t == 4:
                        split_lo(l, STAGE_BLOCKS * (s + 1) + 1, SLOT)
                low(KT - 1)

            def hidden(l, s, g):
                group, last = GROUP0[s], STAGE_BLOCKS * s + 1
                for i in range(2):
                    f = 2 * i + 1
                    n = l * (2 * FT) + (s // 2) * FT + 2 * g + i
                    dve.wait_ge(quarter, quarters(l, last, f, g, UP_BLOCKS))
                    dve.wait_ge(bank_read[f - 1], read_in(l, group, g))
                    v.tensor_tensor(silu[:, i, :], silu[:, i, :], bank[f][:, :], ALU.mult).then_inc(bank_read[f], 1)
                    dve.wait_ge(act_hi_done, n + 1)
                    v.tensor_tensor(tile(act_lo, 2 * g + i), silu[:, i, :], tile(act_hi, 2 * g + i).bitcast(F32),
                                    ALU.subtract).then_inc(act_ready, 1)

            def ffn(l, s):
                base = STAGE_BLOCKS * s
                split_lo(l, base + 2, SLOT)
                hidden(l, s, 0)
                with dve.Fori(1, UP_GROUPS) as g:
                    split_lo(l, base + 1, SLOT, g, UP_BLOCKS)
                    split_lo(l, base + 2, SLOT, g, UP_BLOCKS)
                    hidden(l, s, g)
                dve.wait_ge(quarter, quarters(l, base + DOWN0 - 1, TILE_N - 1))
                clear_sums(l, s)
                coefficients(l, s)
                with dve.Fori(0, DOWN_GROUPS) as g:
                    for b in range(DOWN_BLOCKS):
                        size = DOWN_KS[(b + 1) % DOWN_BLOCKS] * 512
                        split_lo(l, base + DOWN0 + b + 1, size, g, DOWN_BLOCKS)
                    residual(l, s, GROUP0[s] + UP_GROUPS, base + DOWN0 + DOWN_BLOCKS - 1, g, DOWN_BLOCKS)
                layer_norm(l, s)

            def log_decays(l):
                for h in range(HEADS):
                    dve.wait_ge(log_act, at(l, LOG_ACT, f"ln{h}"))
                    v.scalar_tensor_tensor(out=zk[:, h, :], in0=zk[:, h, :], scalar=0.0, in1=tmp[:, h, :],
                                           op0=ALU.min, op1=ALU.subtract).then_inc(log_a_done, 1)

            def prepare(l, h):
                turn = l * HEADS + h
                t0, t1, t2, b = (tmp[:, i, :] for i in range(4))
                q, k = qk[:, h, 0, :], qk[:, h, 1, :]

                def step(ins):
                    ins.then_inc(prep_dve, 1)

                def wait(sem_, steps, name):
                    dve.wait_ge(sem_, at(turn, steps, name))
                dve.wait_ge(log_a_done, (l + 1) * HEADS)
                for n in range(N_CHUNK):
                    cols = slice(n * CHUNK, (n + 1) * CHUNK)
                    ins = v.tensor_tensor_scan(tmp[:, 3, cols], ones[:, 0:CHUNK], zk[:, h, cols], 0.0, ALU.mult, ALU.add)
                step(ins)
                wait(prep_dve, PREP_DVE, "b")
                b3 = b.rearrange("p (n c) -> p n c", c=CHUNK)
                step(v.tensor_tensor(t2.rearrange("p (n c) -> p n c", c=CHUNK),
                                     b3[:, :, CHUNK - 1:CHUNK].to_broadcast([P, N_CHUNK, CHUNK]), b3, ALU.subtract))
                wait(prep_act, PREP_ACT, "exp_end")
                step(v.tensor_tensor(zk[:, h, :], k, t2, ALU.mult))
                step(v.scalar_tensor_tensor(out=q, in0=q, scalar=float(DK // HEADS) ** -0.5, in1=t0,
                                            op0=ALU.mult, op1=ALU.mult))
                step(v.tensor_copy(decay[:, h, :], tmp[:, 0, CHUNK - 1::CHUNK]))
                step(v.tensor_tensor(k, k, t1, ALU.mult))
                wait(prep_dve, PREP_DVE, "kt")

            def normalise(l, h):
                turn = l * HEADS + h
                rstd_h = tmp[:, 4, :]
                for d in range(2):
                    o = tmp[:, 2 * (h % 2) + d, :]
                    t = 2 * h + d
                    v.tensor_tensor(o, o, zk[:, h, :], ALU.subtract).then_inc(norm_dve, 1)
                    if d == 0:
                        dve.wait_ge(norm_act, at(turn, NORM_ACT, "rstd"))
                    dve.wait_ge(norm_dve, at(turn, NORM_DVE, f"c{d}"))
                    v.tensor_tensor(o, o, rstd_h, ALU.mult).then_inc(norm_dve, 1)
                    dve.wait_ge(norm_dve, at(turn, NORM_DVE, f"n{d}"))
                    dve.wait_ge(bank_read[t % TILE_N], read_in(l, GROUP0[1] + MIX_GROUP[f"r{t // TILE_N}"]))
                    v.scalar_tensor_tensor(out=o, in0=o, scalar=layer_p[:, t:t + 1], in1=r_act[:, t, :],
                                           op0=ALU.mult, op1=ALU.mult).then_inc(norm_dve, 1)
                for d in range(2):
                    t = 2 * h + d
                    dve.wait_ge(o_hi_done, l * KT + t + 1)
                    v.tensor_tensor(o_lo[:, t, :], tmp[:, 2 * (h % 2) + d, :], o_hi[:, t, :].bitcast(F32),
                                    ALU.subtract).then_inc(norm_dve, 1)

            def attend(l, i):
                for what, h in gla_slot(i):
                    turn = l * HEADS + h
                    if what == "sc":
                        dve.wait_ge(state_pe, at(turn, STATE_PE, "sc"))
                        v.memset(touch_v[:, :], 0.0)
                        v.copy_predicated(sc[:, :].rearrange("p (a d) -> p a d", d=P),
                                          mask[:, :].unsqueeze(1).to_broadcast([P, PAIRS, P]),
                                          B_T[:, :].rearrange("p (a d) -> p a d", d=P)).then_inc(state_dve, 1)
                    elif what[:2] == "kv":
                        dve.wait_ge(state_pe, at(turn, STATE_PE, what))
                        n = int(what[2])
                        new = (B_KV, B_T)[n % 2][:, 0:HV]
                        if n == 0:
                            ins = v.tensor_copy(state[:, 1, :], new)
                        else:
                            dve.wait_ge(state_dve, at(turn, STATE_DVE, f"S{n}"))
                            ins = v.scalar_tensor_tensor(out=state[:, n + 1, :], in0=state[:, n, :],
                                                         scalar=decay[:, h, n:n + 1], in1=new,
                                                         op0=ALU.mult, op1=ALU.add)
                        ins.then_inc(state_dve, 1)
                    elif what == "o1":
                        dve.wait_ge(norm_act, at(turn, NORM_ACT, "o1"))
                        o0 = 2 * (h % 2)
                        v.tensor_tensor(zk[:, h, :], tmp[:, o0, :], tmp[:, o0 + 1, :], ALU.add).then_inc(norm_dve, 1)
                        dve.wait_ge(norm_act, at(turn, NORM_ACT, "q1"))
                        v.tensor_tensor(tmp[:, 4, :], tmp[:, 4, :], stat[:, :], ALU.add).then_inc(norm_dve, 1)
                    elif what == "stats":
                        dve.wait_ge(norm_act, at(turn, NORM_ACT, "msq"))
                        v.scalar_tensor_tensor(out=tmp[:, 4, :], in0=B_T[:, :], scalar=1.0 / HV, in1=stat[:, :],
                                               op0=ALU.mult, op1=ALU.subtract).then_inc(norm_dve, 1)
                        dve.wait_ge(norm_dve, at(turn, NORM_DVE, "var"))
                        v.tensor_scalar(tmp[:, 4, :], tmp[:, 4, :], 0.0, LN_EPS, ALU.max, ALU.add).then_inc(norm_dve, 1)

            def pool_windows(l):
                done = l * WINDOW_STEPS
                dve.wait_ge(norm_dve, at(l * HEADS + HEADS - 1, NORM_DVE, "lo1"))
                for g, w in enumerate(WINDOWS):
                    u = u_p[:, g, :]
                    s = u
                    for i in range(g + 1):
                        step = 1 << i
                        to = win[:, i % 2, :]
                        v.tensor_tensor(to[:, step:S], s[:, step:S], s[:, 0:S - step], ALU.add).then_inc(win_dve, 1)
                        v.tensor_copy(to[:, 0:step], s[:, 0:step]).then_inc(win_dve, 1)
                        done += 2
                        dve.wait_ge(win_dve, done)
                        s = to
                    to = win[:, (g + 1) % 2, :]
                    v.tensor_scalar(to[:, w - 1:S], s[:, w - 1:S], 1.0 / w, None, ALU.mult).then_inc(win_dve, 1)
                    v.tensor_tensor(to[:, 0:w - 1], s[:, 0:w - 1], cinv[:, 0:w - 1], ALU.mult).then_inc(win_dve, 1)
                    dve.wait_ge(win_dve, done + 2)
                    v.tensor_tensor(u, to, u, ALU.subtract).then_inc(win_dve, 1)
                    done += 3
                    dve.wait_ge(win_dve, done)

            def mixer(l):
                v.memset(sc[:, :], 0.0).then_inc(sc_zero, 1)
                v.tensor_copy(layer_p[:, :], params[:, bass.ds(l * PER_LAYER + P_LAYER, PER_LAYER)])\
                    .then_inc(layer_copied, 1)
                dve.wait_ge(sc_zero, l + 1)
                dve.wait_ge(layer_copied, l + 1)
                nb = STAGE_BLOCKS
                for name, n, size, _ in MIX:
                    half = int(name[-1]) if name[-1].isdigit() else 0
                    group = GROUP0[1] + MIX_GROUP[name]
                    if name == "z":
                        for h in range(HEADS):
                            dve.wait_ge(z_pe, l * HEADS + h + 1 + HEADS)
                            v.tensor_scalar(zk[:, h, :], bank[h][:, :],
                                            layer_p[:, KT + POOL_GROUPS + h:KT + POOL_GROUPS + h + 1], None,
                                            ALU.add).then_inc(bank_read[h], 1)
                            dve.wait_ge(bank_read[h], read_in(l, group))
                    if name == "out0":
                        dve.wait_ge(quarter, quarters(l, STAGE_BLOCKS + MIX_FIRST["gp1"] + 1, TILE_N - 1))
                        clear_sums(l, 1)
                        coefficients(l, 1)
                    for b in range(n):
                        j = nb - STAGE_BLOCKS
                        if j > 0:
                            split_lo(l, nb + 1, MIX_SIZE[j + 1])
                        nb += 1
                        last = b == n - 1
                        for h in V_BLOCK_HEADS[2 * half + b] if name[0] == "v" else ():
                            if h is None:
                                log_decays(l)
                            else:
                                prepare(l, h)
                        if name in GLA_GROUPS:
                            h = (GLA_GROUPS[name] + TILE_N * b) // 4 - 2
                            if h >= 0:
                                normalise(l, h)
                            for f in range(TILE_N):
                                attend(l, GLA_GROUPS[name] + TILE_N * b + f)
                        if name == "gg0" and b == 0:
                            for f in range(TILE_N):
                                dve.wait_ge(bank_read[f], read_in(l, GROUP0[1] + MIX_GROUP["u"]))
                            pool_windows(l)
                        if name == "gg0" and last:
                            for g in range(POOL_GROUPS):
                                dve.wait_ge(p_hi_done, l * POOL_GROUPS + g + 1)
                                v.tensor_tensor(p_lo[:, g, :], u_p[:, g, :], p_hi[:, g, :].bitcast(F32),
                                                ALU.subtract).then_inc(p_ready, 1)
                        if name == "wp":
                            for f in range(TILE_N):
                                dve.wait_ge(quarter, quarters(l, nb - 1, f))
                                v.tensor_scalar(u_p[:, f, :], bank[f][:, :], layer_p[:, KT + f:KT + f + 1], None,
                                                ALU.mult).then_inc(bank_read[f], 1)
                            for f in range(TILE_N):
                                dve.wait_ge(pooled_hi_done, l * POOL_GROUPS + f + 1)
                                v.tensor_tensor(pooled_lo[:, f, :], u_p[:, f, :], pooled_hi[:, f, :].bitcast(F32),
                                                ALU.subtract).then_inc(pooled_ready, 1)
                        if name[:2] == "yg" and last:
                            for f in range(TILE_N):
                                dve.wait_ge(bank_read[f], free_for(l, group))
                                dve.wait_ge(quarter, quarters(l, nb - 1, f))
                                v.tensor_tensor(sg[:, f, :], sg[:, f, :], bank[f][:, :], ALU.mult)\
                                    .then_inc(bank_read[f], 1)
                        if name[:2] == "yp":
                            for f in range(TILE_N):
                                t = TILE_N * half + f
                                dve.wait_ge(bank_read[f], free_for(l, group))
                                dve.wait_ge(quarter, quarters(l, nb - 1, f))
                                v.tensor_tensor(sp_[:, f, :], sp_[:, f, :], bank[f][:, :], ALU.mult)\
                                    .then_inc(bank_read[f], 1)
                                dve.wait_ge(bank_read[f], read_in(l, group))
                                v.tensor_tensor(sp_[:, f, :], sp_[:, f, :], sg[:, f, :], ALU.add).then_inc(merged, 1)
                                if f:
                                    merge_low(l, t - 1)
                            merge_low(l, t)
                        if name[:3] == "out" and last:
                            residual(l, 1, group - half, nb - 1 - 2 * half, half, 2)
                layer_norm(l, 1)

            def merge_low(l, t):
                dve.wait_ge(m_hi_done, l * KT + t + 1)
                v.tensor_tensor(m_lo[:, t, :], sp_[:, t % TILE_N, :], m_hi[:, t, :].bitcast(F32),
                                ALU.subtract).then_inc(m_ready, 1)

            with dve.Fori(0, DEPTH) as l:
                ffn(l, 0)
                mixer(l)
                ffn(l, 2)

        @block.tensor
        def _(pe):
            mm = nc.tensor.matmul
            pe.sem_inc(quarter, 8)
            pe.sem_inc(ada_red, 2)
            pe.sem_inc(z_pe, HEADS)

            n = N_MOD * KT
            pe.wait_ge(consts, 3)
            pe.wait_ge(in_mod, 16 * 2)
            nc.tensor.transpose(bank[5][:, 0:n + KT], stage_rows[0:n + KT, 1, :], ident[0:n + KT, 0:n + KT])\
                .then_inc(small_t, 1)
            pe.wait_ge(in_x, 16 * PAIRS)
            for t in range(KT):
                if t >= TILE_N:
                    pe.wait_ge(x_r, t - TILE_N + 1)
                for a in range(PAIRS):
                    ins = nc.tensor.transpose(bank[t % TILE_N][:, a * P:(a + 1) * P],
                                              x_tok[:, a, t * P:(t + 1) * P], ident[:, :])
                ins.then_inc(x_t, 1)
            pe.wait_ge(c_ready, 1)
            for i in (0, 1, 2, 3):
                if i == 3:
                    pe.wait_ge(in_small, 16 * (2 + 3 * DEPTH + 1))
                    nc.tensor.transpose(bank[4][:, 0:P], stage_rows[:, 0, :], ident[:, :]).then_inc(small_t, 1)
                    nc.tensor.transpose(bank[6][:, 0:n], stage_rows[0:n, 2, :], ident[0:n, 0:n]).then_inc(small_t, 1)
                if i in ADA_DVE:
                    pe.wait_ge(ada0_mul, (ADA_DVE.index(i) + 1) * KT)
                else:
                    pe.wait_ge(in_ada[i], 16)
                for t in range(4):
                    col = KT + 4 * i + t
                    if i in ADA_DVE:
                        ins = mm(B_ADA[:, col:col + 1], ada_start[:, i, 0, t * P:(t + 1) * P], ones[:, 0:1],
                                 start=True, stop=True)
                    else:
                        for k in range(KT):
                            ins = mm(B_ADA[:, col:col + 1], ada_start[:, i, k, t * P:(t + 1) * P],
                                     c_act[:, k:k + 1], start=(k == 0), stop=(k == KT - 1))
                ins.then_inc(ada0, 1)

            def product(out_, w_, a_, start, stop, moving_w=False):
                (w1, w0), (a1, a0) = w_, a_
                if moving_w:
                    (w1, w0), (a1, a0) = (a1, a0), (w1, w0)
                mm(out_, w1, a1, start=start, stop=False)
                mm(out_, w1, a0, start=False, stop=False)
                return mm(out_, w0, a1, start=False, stop=stop)

            def weights(slot, k, f, width=512):
                c = slice(k * width + f * P, k * width + f * P + min(P, width))
                return wh[:, slot, c], wl[:, slot, c]

            def run_block(l, nb, a, ks, group, first, last, g=0, per=0, cols=(0, 1, 2, 3), k_outer=None, tokens=False,
                          behind=None):
                slot = nb % 2
                pe.wait_ge(w_lo, split_done(l, nb, g, per))

                def one(f, k):
                    start, stop = first and k == 0, last and k == ks - 1
                    if start:
                        pe.wait_ge(bank_read[f], free_for(l, group, g))
                    if tokens:
                        hi, lo = a(k)
                        at_f = slice(f * P, (f + 1) * P)
                        w = (wh[:, slot, k * 512:(k + 1) * 512], wl[:, slot, k * 512:(k + 1) * 512])
                        return product(bank[f][:, :], w, (hi[:, at_f], lo[:, at_f]), start, stop, moving_w=True)
                    return product(bank[f][:, :], weights(slot, k, cols[f]), a(k), start, stop)

                if k_outer:
                    for k in range(ks):
                        k_outer(k)
                        for f in range(TILE_N):
                            ins = one(f, k)
                            if k == ks - 1:
                                ins.then_inc(quarter, 1)
                    return
                for f in range(TILE_N):
                    for k in range(ks):
                        ins = one(f, k)
                    ins.then_inc(quarter, 1)
                    if behind:
                        behind(f)

            def h(b):
                return lambda k: (h_hi[:, 4 * b + k, :], h_lo[:, 4 * b + k, :])

            def h_there(l, s, b):
                return lambda k: pe.wait_ge(h_ready, (l * 3 + s) * KT + 4 * b + k + 1)

            def ada_pair(l, s, pair):
                if isinstance(pair, int) and pair == 0:
                    pe.wait_ge(coef, at(l * 3 + s, COEF, "mods"))
                for i in range(2):
                    pe.wait_ge(ada_step, l * (12 * ADA) + pair * 8 + 4 * (s * ADA + i) + 4)
                    mm(B_ADA[:, bass.ds(pair * 2 + i, 1)], ada[:, i, 0, :], ones[:, 0:1],
                       start=True, stop=True).then_inc(ada_red, 1)

            def norm_sums(l, s):
                pe.wait_ge(ln_sum, (l * 3 + s + 1) * (2 * KT) + 3)
                mm(B_OUT[:, :], ones[:, :], ln_acc[:, :], start=True, stop=True).then_inc(ln_pe, 1)
                pe.wait_ge(ln_sum, (l * 3 + s + 1) * (2 * KT) + 4)
                mm(B_KV[:, :], ones[:, :], ln_accq[:, :], start=True, stop=True).then_inc(ln_pe, 1)

            def ffn(l, s):
                base, group = STAGE_BLOCKS * s, GROUP0[s]
                up_cols = (0, 2, 1, 3)
                ada_pair(l, s, 0)
                for b in range(UP_BLOCKS):
                    run_block(l, base + b, h(b), 4, group, b == 0, b == 1, cols=up_cols, k_outer=h_there(l, s, b))
                ada_pair(l, s, 1)
                with pe.Fori(1, UP_GROUPS) as g:
                    for b in range(UP_BLOCKS):
                        run_block(l, base + b, h(b), 4, group, b == 0, b == 1, g, UP_BLOCKS, cols=up_cols)
                    ada_pair(l, s, g + 1)
                with pe.Fori(0, DOWN_GROUPS) as g:
                    k0 = 0
                    for b, ks in enumerate(DOWN_KS):
                        pe.wait_ge(act_ready, l * (2 * FT) + (s // 2) * FT + k0 + ks + 2)
                        run_block(l, base + DOWN0 + b, lambda k, k0=k0: (act_hi[:, k0 + k, :], act_lo[:, k0 + k, :]), ks,
                                  group + UP_GROUPS, b == 0, b == DOWN_BLOCKS - 1, g, DOWN_BLOCKS)
                        k0 += ks
                norm_sums(l, s)

            def attend(l, i):
                for what, hd in gla_slot(i):
                    turn = l * HEADS + hd
                    q, k, kend = qk[:, hd, 0, :], qk[:, hd, 1, :], zk[:, hd, :]
                    if what == "kT":
                        pe.wait_ge(prep_dve, at(turn, PREP_DVE, "kt"))
                        if hd >= 2:
                            pe.wait_ge(norm_dve, at(turn - 2, NORM_DVE, "var"))
                        for a in range(PAIRS):
                            ins = nc.tensor.transpose(B_T[:, a * P:(a + 1) * P], kend[:, a * P:(a + 1) * P], ident[:, :])
                        ins.then_inc(state_pe, 1)
                    elif what == "sc":
                        pe.wait_ge(kend_read, turn + 1)
                        for a in range(PAIRS):
                            at_a = slice(a * P, (a + 1) * P)
                            ins = mm(B_T[:, at_a], k[:, at_a], q[:, at_a], start=True, stop=True)
                        ins.then_inc(state_pe, 1)
                    elif what[:2] == "kv":
                        n = int(what[2])
                        if n:
                            pe.wait_ge(state_dve, at(turn, STATE_DVE, f"S{n - 1}" if n > 1 else "sc"))
                        rows = slice(n % 2 * CHUNK, (n % 2 + 1) * CHUNK)
                        mm((B_KV, B_T)[n % 2][:, 0:HV], kend_tok[rows, n // 2, :],
                           v_tok[rows, n // 2, hd * HV:(hd + 1) * HV], start=True, stop=True).then_inc(state_pe, 1)
                    elif what in ("o0", "o1"):
                        d = int(what[1])
                        pe.wait_ge(state_dve, at(turn, STATE_DVE, "S7"))
                        if d:
                            pe.wait_ge(norm_act, at(turn, NORM_ACT, "o0"))
                        elif hd:
                            pe.wait_ge(norm_act, at(turn - 1, NORM_ACT, "msq"))
                        cols = slice(hd * HV + d * P, hd * HV + (d + 1) * P)
                        for a in range(PAIRS):
                            at_a = slice(a * P, (a + 1) * P)
                            mm(B_OUT[:, at_a], v_tok[:, a, cols], sc[:, at_a], start=True, stop=False)
                            for n in (2 * a, 2 * a + 1):
                                if n:
                                    at_n = slice(n * CHUNK, (n + 1) * CHUNK)
                                    ins = mm(B_OUT[:, at_n], state[:, n, d * P:(d + 1) * P], q[:, at_n],
                                             start=False, stop=n == 2 * a + 1)
                        ins.then_inc(out_pe, 1)
                    elif what == "stats":
                        pe.wait_ge(norm_dve, at(turn, NORM_DVE, "osum"))
                        mm(B_OUT[:, :], ones[:, :], zk[:, hd, :], start=True, stop=True).then_inc(out_pe, 1)
                        if hd < HEADS - 1:
                            pe.wait_ge(state_dve, at(turn + 1, STATE_DVE, "S6"))
                        pe.wait_ge(norm_dve, at(turn, NORM_DVE, "sqsum"))
                        mm(B_T[:, :], ones[:, :], tmp[:, 4, :], start=True, stop=True).then_inc(out_pe, 1)

            def mixer(l):
                nb = STAGE_BLOCKS
                for name, n, size, pair in MIX:
                    group = GROUP0[1] + MIX_GROUP[name]
                    if name == "a":
                        pe.wait_ge(w_lo, split_done(l, nb))
                        for k in range(KT):
                            w = tuple(t[:, nb % 2, k * RANK:(k + 1) * RANK] for t in (wh, wl))
                            ins = product(B_T[0:RANK, :], w, (h_hi[:, k, :], h_lo[:, k, :]), k == 0, k == KT - 1)
                            if k % 2:
                                ins.then_inc(quarter, 1)
                        nb += 1
                        continue
                    if name == "z":
                        pe.wait_ge(a_act, l + 1)
                        pe.wait_ge(in_alpha, l * 16 + 16)
                        for hd in range(HEADS):
                            pe.wait_ge(bank_read[hd], free_for(l, group))
                            mm(bank[hd][:, :], alpha_w[:, hd * P:(hd + 1) * P], a_sb[:, :], start=True, stop=True)\
                                .then_inc(z_pe, 1)
                        continue
                    if name == "wp":
                        pe.wait_ge(w_lo, split_done(l, nb))
                        for g in range(POOL_GROUPS):
                            pe.wait_ge(bank_read[g], free_for(l, group))
                            pe.wait_ge(p_ready, l * POOL_GROUPS + g + 1)
                            product(bank[g][:, :], weights(nb % 2, g, 0, P), (p_hi[:, g, :], p_lo[:, g, :]),
                                    True, True).then_inc(quarter, 1)
                        nb += 1
                        continue
                    if name == "yg0":
                        pe.wait_ge(norm_dve, at(l * HEADS + HEADS - 1, NORM_DVE, "lo1"))
                    if name == "yp0":
                        pe.wait_ge(pooled_ready, l * POOL_GROUPS + POOL_GROUPS)
                    for b in range(n):
                        behind = k_outer = None
                        a = h(b)
                        if name == "q":
                            k_outer = h_there(l, 1, b)
                        elif name in GLA_GROUPS:
                            def behind(f, i=GLA_GROUPS[name] + TILE_N * b):
                                attend(l, i + f)
                        elif name[:2] == "yg":
                            def a(k, b=b):
                                return o_hi[:, 4 * b + k, :], o_lo[:, 4 * b + k, :]
                        elif name[:2] == "yp":
                            def a(k):
                                return pooled_hi[:, k, :], pooled_lo[:, k, :]
                        elif name[:3] == "out":
                            pe.wait_ge(m_ready, l * KT + 4 * b + 4)

                            def a(k, b=b):
                                return m_hi[:, 4 * b + k, :], m_lo[:, 4 * b + k, :]
                        run_block(l, nb, a, 4, group, b == 0, b == n - 1, k_outer=k_outer, tokens=name[0] == "v",
                                  behind=behind)
                        nb += 1
                    if pair is not None:
                        ada_pair(l, 1, pair)
                norm_sums(l, 1)

            with pe.Fori(0, DEPTH) as l:
                ffn(l, 0)
                mixer(l)
                ffn(l, 2)
            for t in range(KT):
                pe.wait_ge(ln_act, at(3 * DEPTH - 1, LN_ACT, f"x{t}"))
                if t >= TILE_N:
                    pe.wait_ge(out_r, t - TILE_N + 1)
                for a in range(PAIRS):
                    ins = nc.tensor.transpose(bank[t % TILE_N][:, a * P:(a + 1) * P], xT[:, t, a * P:(a + 1) * P],
                                              ident[:, :])
                ins.then_inc(out_t, 1)


_INS = ["x", "c", "w_ada", "b_ada", "ffn1_up", "ffn1_down", "w_in", "w_alpha", "b_alpha", "gla_norm_g", "w_proj_gla",
        "w_pool", "pool_scale", "w_proj_pool", "w_out", "ffn2_up", "ffn2_down", "ln_g", "ln_b"]


def kernel(**inputs):
    import numpy as _np
    import concourse.bacc as _bacc
    from concourse import mybir as _mybir
    from concourse.bass_utils import run_bass_kernel_spmd as _run

    nc = _bacc.Bacc("TRN2", target_bir_lowering=False, num_devices=1)
    arrays, args = {}, []
    for name in _INS:
        a = _np.ascontiguousarray(inputs[name])
        arrays[f"in_{name}_dram"] = a
        args.append(nc.dram_tensor(f"in_{name}_dram", a.shape, _mybir.dt.from_np(a.dtype), kind="ExternalInput").ap())
    args.append(nc.dram_tensor("out_dram", (1, S, D), _mybir.dt.float32, kind="ExternalOutput").ap())
    trunk(nc, *args)
    r = _run(nc, [arrays], core_ids=[0])
    return r.results[0]["out_dram"]
```
